# Optimizing a Trainium2 kernel written in Bass

```python
import jax, jax.numpy as jnp
from jax import lax
import numpy as np

D_MODEL = 1024
BATCH = 1
SEQ = 512
DEPTH = 2

RMS_EPS = 1e-6
LN_EPS = 1e-5
N_EVEN = (DEPTH + 1) // 2
N_ODD = DEPTH // 2

GLA_WIDTH = D_MODEL // 2
GLA_HEADS = 4
GLA_DK = GLA_WIDTH // 2 // GLA_HEADS
GLA_DV = GLA_WIDTH // GLA_HEADS
GLA_KEY = GLA_HEADS * GLA_DK
GLA_GATE_RANK = 16
GLA_TAU = 16.0
GLA_CHUNK = 64
SGU_WIDTH = D_MODEL - GLA_WIDTH
SGU_GROUPS = 4
SGU_GROUP_DIM = SGU_WIDTH // SGU_GROUPS
SGU_CHUNK = 128
EVEN_SPLITS = (GLA_KEY, GLA_KEY, GLA_WIDTH, GLA_WIDTH, GLA_GATE_RANK, SGU_WIDTH, SGU_WIDTH)
EVEN_IN = sum(EVEN_SPLITS)

RWKV_WIDTH = D_MODEL // 2
RWKV_HEAD = 64
RWKV_HEADS = RWKV_WIDTH // RWKV_HEAD
RWKV_DECAY_RANK = 32
RWKV_AAA_RANK = 32
RWKV_GATE_RANK = 96
RWKV_GN_EPS = 64e-5
RWKV_SPLITS = (RWKV_WIDTH, RWKV_WIDTH, RWKV_WIDTH, RWKV_DECAY_RANK, RWKV_AAA_RANK, RWKV_GATE_RANK)
RWKV_IN = sum(RWKV_SPLITS)
CONV_WIDTH = D_MODEL - RWKV_WIDTH
CONV_KERNEL = 31
ODD_IN = RWKV_IN + 2 * CONV_WIDTH

D_FF = 4 * D_MODEL

kernel_name = "hybrid_gla_sgu_rwkv7_conformer_trunk"

def _split(h, sizes):
    idx = [int(i) for i in np.cumsum(sizes)[:-1]]
    return jnp.split(h, idx, axis=-1)

def _rmsnorm(x, g):
    xf = x.astype(jnp.float32)
    y = xf * lax.rsqrt(jnp.mean(xf * xf, axis=-1, keepdims=True) + RMS_EPS)
    return (y * g.astype(jnp.float32)).astype(x.dtype)

def _layernorm(x, g, b, eps):
    mu = jnp.mean(x, axis=-1, keepdims=True)
    var = jnp.mean(jnp.square(x - mu), axis=-1, keepdims=True)
    return (x - mu) * lax.rsqrt(var + eps) * g.astype(jnp.float32) + b.astype(jnp.float32)

def _token_shift(x):
    return jnp.pad(x[:, :-1], ((0, 0), (1, 0), (0, 0)))

def _gla(q, k, v, g, alpha_lr, w_alpha2, b_alpha, gn_gain):
    B, T, _ = q.shape
    N = T // GLA_CHUNK
    log_a = jax.nn.log_sigmoid(alpha_lr @ w_alpha2.astype(jnp.float32) + b_alpha.astype(jnp.float32)) / GLA_TAU

    def heads(t, d):
        return t.reshape(B, N, GLA_CHUNK, GLA_HEADS, d).transpose(0, 3, 1, 2, 4)

    qh = heads(q, GLA_DK) * (GLA_DK ** -0.5)
    kh = heads(k, GLA_DK)
    vh = heads(v, GLA_DV)
    b = jnp.cumsum(heads(log_a, GLA_DK), axis=3)
    b_last = b[:, :, :, -1:, :]
    q_dec = qh * jnp.exp(b)
    k_dec = kh * jnp.exp(-b)
    k_state = kh * jnp.exp(b_last - b)
    mask = jnp.tril(jnp.ones((GLA_CHUNK, GLA_CHUNK), dtype=bool))
    att = jnp.where(mask, jnp.einsum('bhncd,bhnsd->bhncs', q_dec, k_dec), 0.0)
    o_intra = jnp.einsum('bhncs,bhnsv->bhncv', att, vh)

    def step(S, inp):
        qd, ks, vv, dl = inp
        o = jnp.einsum('bhcd,bhdv->bhcv', qd, S)
        S = S * dl[..., None] + jnp.einsum('bhcd,bhcv->bhdv', ks, vv)
        return S, o

    xs = (jnp.moveaxis(q_dec, 2, 0), jnp.moveaxis(k_state, 2, 0), jnp.moveaxis(vh, 2, 0),
          jnp.moveaxis(jnp.exp(b_last[:, :, :, 0, :]), 2, 0))
    S0 = jnp.zeros((B, GLA_HEADS, GLA_DK, GLA_DV), jnp.float32)
    _, o_inter = lax.scan(step, S0, xs)
    o = o_intra + jnp.moveaxis(o_inter, 0, 2)
    o = o * lax.rsqrt(jnp.mean(o * o, axis=-1, keepdims=True) + RMS_EPS)
    o = o.transpose(0, 2, 3, 1, 4).reshape(B, T, GLA_WIDTH) * gn_gain.astype(jnp.float32)
    return o * jax.nn.silu(g)

def _sgu(u, sv, ln_g, ln_b, w_s, b_s):
    B, T, _ = u.shape
    N = T // SGU_CHUNK
    u = jax.nn.gelu(u)
    sv = _layernorm(jax.nn.gelu(sv), ln_g, ln_b, LN_EPS)
    vh = sv.reshape(B, N, SGU_CHUNK, SGU_GROUPS, SGU_GROUP_DIM)
    mask = jnp.tril(jnp.ones((SGU_CHUNK, SGU_CHUNK), dtype=bool))
    w = jnp.where(mask[None], w_s.astype(jnp.float32), 0.0)
    s = jnp.einsum('gts,bnsgc->bntgc', w, vh) + b_s.astype(jnp.float32).T[:, :, None]
    return u * s.reshape(B, T, SGU_WIDTH)

def _rwkv7_scan(r, w, k, v, kk, a):
    B, T, H, N = r.shape

    def step(S, inp):
        r_t, w_t, k_t, v_t, kk_t, a_t = inp
        sa = -jnp.einsum('bhvk,bhk->bhv', S, kk_t)
        S = (S * w_t[:, :, None, :] + sa[..., None] * (kk_t * a_t)[:, :, None, :]
             + v_t[..., None] * k_t[:, :, None, :])
        return S, jnp.einsum('bhvk,bhk->bhv', S, r_t)

    xs = tuple(jnp.moveaxis(t, 1, 0) for t in (r, w, k, v, kk, a))
    _, y = lax.scan(step, jnp.zeros((B, H, N, N), jnp.float32), xs)
    return jnp.moveaxis(y, 0, 1)

def _rwkv7(h, mu, w0, w2, a0, a2, g2, k_k, k_a, r_k, gn_g, gn_b):
    B, T, _ = h.shape
    f32 = jnp.float32
    h = h + (_token_shift(h) - h) * mu.astype(f32)
    r, k, v, xw, xa, xg = _split(h, RWKV_SPLITS)
    wlog = -jax.nn.softplus(-(w0.astype(f32) + jnp.tanh(xw) @ w2.astype(f32))) - 0.5
    decay = jnp.exp(-jnp.exp(wlog))
    a = jax.nn.sigmoid(a0.astype(f32) + xa @ a2.astype(f32))
    g = jax.nn.sigmoid(xg) @ g2.astype(f32)
    hd = lambda t: t.reshape(B, T, RWKV_HEADS, RWKV_HEAD)
    kk = hd(k * k_k.astype(f32))
    kk = kk / jnp.maximum(jnp.sqrt(jnp.sum(kk * kk, axis=-1, keepdims=True)), 1e-12)
    k = k * (1.0 + (a - 1.0) * k_a.astype(f32))
    rh, kh, vh = hd(r), hd(k), hd(v)
    y = _rwkv7_scan(rh, hd(decay), kh, vh, kk, hd(a))
    mu_y = jnp.mean(y, axis=-1, keepdims=True)
    var_y = jnp.mean(jnp.square(y - mu_y), axis=-1, keepdims=True)
    y = ((y - mu_y) * lax.rsqrt(var_y + RWKV_GN_EPS)).reshape(B, T, RWKV_WIDTH)
    y = y * gn_g.astype(f32) + gn_b.astype(f32)
    bonus = jnp.sum(rh * kh * r_k.astype(f32), axis=-1, keepdims=True) * vh
    y = y + bonus.reshape(B, T, RWKV_WIDTH)
    return y * g

def _conformer_conv(h, conv_w, conv_b, ln_g, ln_b):
    a, gate = _split(h, (CONV_WIDTH, CONV_WIDTH))
    z = a * jax.nn.sigmoid(gate)
    z = jnp.pad(z, ((0, 0), (CONV_KERNEL - 1, 0), (0, 0)))
    y = lax.conv_general_dilated(z, conv_w.astype(jnp.float32)[:, None, :], window_strides=(1,),
                                 padding='VALID', dimension_numbers=('NWC', 'WIO', 'NWC'),
                                 feature_group_count=CONV_WIDTH)
    y = y + conv_b.astype(jnp.float32)
    return jax.nn.silu(_layernorm(y, ln_g, ln_b, LN_EPS))

def setup_inputs(seed: int = 0) -> dict:
    key = jax.random.key(seed)
    keys = jax.random.split(key, 40)
    f32 = jnp.float32
    D = D_MODEL

    def nrm(i, shape, scale):
        return scale * jax.random.normal(keys[i], shape, f32)

    def gain(i, shape):
        return 1.0 + nrm(i, shape, 0.05)

    w0_ramp = jnp.linspace(-6.5, -1.5, RWKV_WIDTH, dtype=f32)
    return {
        "x": nrm(0, (BATCH, SEQ, D), 1.0),
        "norm_mix": gain(1, (DEPTH, D)),
        "norm_ffn": gain(2, (DEPTH, D)),
        "w_up": nrm(3, (DEPTH, D, D_FF), D ** -0.5),
        "w_down": nrm(4, (DEPTH, D_FF, D), D_FF ** -0.5),
        "norm_final": gain(5, (D,)),
        "even_w_in": nrm(6, (N_EVEN, D, EVEN_IN), D ** -0.5),
        "even_w_out": nrm(7, (N_EVEN, D, D), D ** -0.5),
        "gla_w_alpha2": nrm(8, (N_EVEN, GLA_GATE_RANK, GLA_KEY), GLA_GATE_RANK ** -0.5),
        "gla_b_alpha": nrm(9, (N_EVEN, GLA_KEY), 0.5),
        "gla_norm": gain(10, (N_EVEN, GLA_WIDTH)),
        "sgu_ln_g": gain(11, (N_EVEN, SGU_WIDTH)),
        "sgu_ln_b": nrm(12, (N_EVEN, SGU_WIDTH), 0.02),
        "sgu_w": nrm(13, (N_EVEN, SGU_GROUPS, SGU_CHUNK, SGU_CHUNK), SGU_CHUNK ** -0.5),
        "sgu_b": gain(14, (N_EVEN, SGU_GROUPS, SGU_CHUNK)),
        "odd_w_in": nrm(15, (N_ODD, D, ODD_IN), D ** -0.5),
        "odd_w_out": nrm(16, (N_ODD, D, D), D ** -0.5),
        "rwkv_mu": jax.random.uniform(keys[17], (N_ODD, RWKV_IN), f32),
        "rwkv_w0": w0_ramp[None, :] + nrm(18, (N_ODD, RWKV_WIDTH), 0.1),
        "rwkv_w2": nrm(19, (N_ODD, RWKV_DECAY_RANK, RWKV_WIDTH), 0.5 * RWKV_DECAY_RANK ** -0.5),
        "rwkv_a0": nrm(20, (N_ODD, RWKV_WIDTH), 0.1),
        "rwkv_a2": nrm(21, (N_ODD, RWKV_AAA_RANK, RWKV_WIDTH), RWKV_AAA_RANK ** -0.5),
        "rwkv_g2": nrm(22, (N_ODD, RWKV_GATE_RANK, RWKV_WIDTH), RWKV_GATE_RANK ** -0.5),
        "rwkv_k_k": 0.85 + nrm(23, (N_ODD, RWKV_WIDTH), 0.05),
        "rwkv_k_a": gain(24, (N_ODD, RWKV_WIDTH)),
        "rwkv_r_k": nrm(25, (N_ODD, RWKV_HEADS, RWKV_HEAD), 0.1),
        "rwkv_gn_g": gain(26, (N_ODD, RWKV_WIDTH)),
        "rwkv_gn_b": nrm(27, (N_ODD, RWKV_WIDTH), 0.02),
        "conv_w": nrm(28, (N_ODD, CONV_KERNEL, CONV_WIDTH), CONV_KERNEL ** -0.5),
        "conv_b": nrm(29, (N_ODD, CONV_WIDTH), 0.02),
        "conv_ln_g": gain(30, (N_ODD, CONV_WIDTH)),
        "conv_ln_b": nrm(31, (N_ODD, CONV_WIDTH), 0.02),
    }

def reference(x, norm_mix, norm_ffn, w_up, w_down, norm_final, even_w_in, even_w_out,
              gla_w_alpha2, gla_b_alpha, gla_norm, sgu_ln_g, sgu_ln_b, sgu_w, sgu_b,
              odd_w_in, odd_w_out, rwkv_mu, rwkv_w0, rwkv_w2, rwkv_a0, rwkv_a2, rwkv_g2,
              rwkv_k_k, rwkv_k_a, rwkv_r_k, rwkv_gn_g, rwkv_gn_b, conv_w, conv_b,
              conv_ln_g, conv_ln_b):
    for layer in range(DEPTH):
        j = layer // 2
        h = _rmsnorm(x, norm_mix[layer])
        if layer % 2 == 0:
            p = (h @ even_w_in[j]).astype(jnp.float32)
            q, k, v, g, alr, u, sv = _split(p, EVEN_SPLITS)
            o_a = _gla(q, k, v, g, alr, gla_w_alpha2[j], gla_b_alpha[j], gla_norm[j])
            o_b = _sgu(u, sv, sgu_ln_g[j], sgu_ln_b[j], sgu_w[j], sgu_b[j])
            m = jnp.concatenate([o_a, o_b], axis=-1).astype(x.dtype)
            x = x + m @ even_w_out[j]
        else:
            p = (h @ odd_w_in[j]).astype(jnp.float32)
            o_c = _rwkv7(p[..., :RWKV_IN], rwkv_mu[j], rwkv_w0[j], rwkv_w2[j], rwkv_a0[j],
                         rwkv_a2[j], rwkv_g2[j], rwkv_k_k[j], rwkv_k_a[j], rwkv_r_k[j],
                         rwkv_gn_g[j], rwkv_gn_b[j])
            o_d = _conformer_conv(p[..., RWKV_IN:], conv_w[j], conv_b[j], conv_ln_g[j], conv_ln_b[j])
            m = jnp.concatenate([o_c, o_d], axis=-1).astype(x.dtype)
            x = x + m @ odd_w_out[j]
        f = jnp.square(jax.nn.relu(_rmsnorm(x, norm_ffn[layer]) @ w_up[layer]))
        x = x + f @ w_down[layer]
    return _rmsnorm(x, norm_final)


_drawn_inputs = setup_inputs


def setup_inputs(seed=0):
    import zlib

    import numpy as np

    out = dict(_drawn_inputs(seed))
    spreads = {}
    factors = {'sgu_ln_g': 3.541,
     'sgu_ln_b': 8.0,
     'sgu_b': 2.71,
     'rwkv_w2': 4.418,
     'rwkv_a0': 6.561,
     'rwkv_k_k': 2.903,
     'rwkv_k_a': 2.846,
     'rwkv_gn_g': 5.918,
     'rwkv_gn_b': 28.963,
     'conv_b': 5.826,
     'conv_ln_g': 3.725,
     'conv_ln_b': 8.0,
     'gla_norm': 3.428}
    for name, (base, spread) in spreads.items():
        noise = np.random.default_rng([zlib.crc32(name.encode()), seed]).standard_normal(out[name].shape)
        drawn = base * np.exp(spread * noise) if base else spread * noise
        out[name] = __import__('jax').numpy.asarray(drawn.astype(out[name].dtype))
    for name, factor in factors.items():
        out[name] = (out[name] * factor).astype(out[name].dtype)
    return out
```

```python
import concourse.bass as bass
from concourse import mybir
from contextlib import ExitStack

import numpy as np

D = 1024
SEQ = 512
FF = 4 * D
P = 128
KD = D // P
TT = SEQ // P
GLA_CHUNK = 64
RW_CHUNK = 128
TAPS = 31
CT = 4
HALF_K = FF // 2 // P
EXP_HALF = float(np.exp(-0.5))
LEVELS = 7

MIX0 = [1, 4, 4, 2, 2, 4, 4, 4, 4, 4, 4]
MIX1 = [2] * 11
OUTP = [2] * 4
MLPC = ([2] * 8 + [1] * 8) * 2
TILES = MIX0 + OUTP + MLPC + MIX1 + OUTP + MLPC
CHUNKS = len(TILES)
ROWS = [0, 2, 4, 3, 14, 15, 5, 7, 6, 1, 16, 17, 8, 10, 9, 18, 19, 11, 13, 12, 20, 21]
FIRST_TILE = [sum(TILES[:n]) for n in range(CHUNKS + 1)]
N_OUT0 = len(MIX0)
N_MLP0 = N_OUT0 + 4
N_MIX1 = N_MLP0 + 32
N_OUT1 = N_MIX1 + len(MIX1)
N_MLP1 = N_OUT1 + 4

COLS = {}
for _name, _n in (("norm_mix0", 8), ("norm_ffn0", 8), ("norm_mix1", 8), ("norm_ffn1", 8), ("norm_final", 8),
                  ("b_alpha", 2), ("gla_norm", 4), ("sgu_b", 4), ("mu_low", 2), ("mu_k", 4), ("mu_v", 4),
                  ("mu_r", 4), ("w0", 4), ("a0", 4), ("k_k", 4), ("k_a", 4), ("r_k", 4), ("gn_g", 4),
                  ("gn_b", 4), ("conv_b", 4), ("ln_g", 4), ("ln_b", 4), ("conv_w", 4 * TAPS)):
    COLS[_name] = (sum(n for _, n in COLS.values()), _n)
NCOL = sum(n for _, n in COLS.values())

MSRC, MCOLS = {}, {}
for _name, _n, _times in [("gla", 128, 2), ("score", 256, 2), ("reset64", 128, 4), ("reset128", 128, 4)] \
        + [(f"lvl{a}{lv}", 64, 4) for lv in range(LEVELS) for a in ("X", "XT")]:
    MSRC[_name] = (sum(n for _, n in MSRC.values()), _n)
    MCOLS[_name] = (sum(n for _, n in MCOLS.values()), _n * _times)
NSRC = sum(n for _, n in MSRC.values())
NMASK = sum(n for _, n in MCOLS.values())


def build(nc, xT_in, weights, cols_in, mats_in, masks_in, sgu_ln_in, sgu_w_in, alpha_w_in, low_w_in, out):
    f32, f32r, u8 = mybir.dt.float32, mybir.dt.float32r, mybir.dt.uint8
    ALU, ACT, AX = mybir.AluOpType, mybir.ActivationFunctionType, mybir.AxisListType
    MUL, ADD, SUB = ALU.mult, ALU.add, ALU.subtract

    ctx = ExitStack()
    with ctx:
        def tensors(stack):
            def sb(name, shape, dt=f32):
                return stack.enter_context(nc.sbuf_tensor(name, shape, dt))
            return sb

        sb = tensors(ctx)
        x = sb("x", [P, KD, SEQ])
        h_hi = sb("h_hi", [P, KD, SEQ], f32r)
        h_lo = sb("h_lo", [P, KD, SEQ], f32r)
        w_raw = sb("w_raw", [P, 2, 2048])
        w_hi = sb("w_hi", [P, 2, 2048], f32r)
        w_lo = sb("w_lo", [P, 2, 2048], f32r)
        cols = sb("cols", [P, NCOL])
        mats = sb("mats", [P, 3, P])
        masks = sb("masks", [P, NMASK], u8)
        low_w = sb("low_w", [P, 2, 512])
        eps = sb("eps", [P, 4])
        IDENT, ONES, BLK = mats[:, 0, :], mats[:, 1, :], mats[:, 2, :]
        EPS_RMS, EPS_LN, EPS_GN, ONE = (eps[:, i:i + 1] for i in range(4))

        def col(name, i=0):
            at = COLS[name][0] + i
            return cols[:, at:at + 1]

        def mask(name, a=0, b=512):
            at = MCOLS[name][0]
            return masks[:, at + a:at + b]

        with ExitStack() as own:
            masks_f = tensors(own)("masks_f", [P, NSRC])
        with ExitStack() as own:
            sb = tensors(own)
            f_hi = sb("f_hi", [P, HALF_K, SEQ], f32r)
            f_lo = sb("f_lo", [P, HALF_K, SEQ], f32r)
            relu = sb("relu", [P, 2, SEQ])
            f_sq = sb("f_sq", [P, SEQ])
            ssq = sb("ssq", [P, SEQ])
            xsq = sb("xsq", [P, SEQ])
            std = sb("std", [P, SEQ])
            rstd = sb("rstd", [P, SEQ])
            hf = sb("hf", [P, 3, SEQ])
        with ExitStack() as own:
            sb = tensors(own)
            sgu_ln = sb("sgu_ln", [P, 2, 512])
            sgu_w = sb("sgu_w", [P, 4, P])
            sgu_wm = sb("sgu_wm", [P, 4, P])
            alpha_w = sb("alpha_w", [16, 256])
            alrT = sb("alrT", [16, SEQ])
            zb = sb("zb", [P, 2, SEQ])
            zl = sb("zl", [P, 2, SEQ])
            bsum = sb("bsum", [P, 2, SEQ])
            e_pos = sb("e_pos", [P, 2, SEQ])
            e_neg = sb("e_neg", [P, 2, SEQ])
            e_end = sb("e_end", [P, 2, SEQ])
            q_dec = sb("q_dec", [P, 2, SEQ])
            k_dec = sb("k_dec", [P, 2, SEQ])
            k_st = sb("k_st", [P, 2, SEQ])
            k_tok = sb("k_tok", [P, TT, 256])
            v_tok = sb("v_tok", [P, TT, 512])
            g_tok = sb("g_tok", [P, TT, 512])
            u_tok = sb("u_tok", [P, TT, 512])
            sv = sb("sv", [P, TT, 512])
            att = sb("att", [P, 2, 512])
            S = sb("S", [P, 8, 2, P])
            o_sb = sb("o_sb", [P, 512])
            o_sq = sb("o_sq", [P, 512])
            o_ms = sb("o_ms", [P, TT, 4])
            o_sd = sb("o_sd", [P, TT, 4])
            o_rs = sb("o_rs", [P, TT, 4])
            ln_st = sb("ln_st", [P, TT, 6])
            ln_mv = sb("ln_mv", [P, TT, 2])
            ln_sd = sb("ln_sd", [P, TT])
            ln_rs = sb("ln_rs", [P, TT])
        with ExitStack() as own:
            sb = tensors(own)
            AR = sb("AR", [P, 2, TT, 2, P])
            bT = sb("bT", [P, SEQ])
            kT = sb("kT", [P, SEQ])
            vT = sb("vT", [P, SEQ])
            vtok = sb("vtok", [P, TT, P])
            btok = sb("btok", [P, TT, P])
            ktok = sb("ktok", [P, TT, P])
            SC = sb("SC", [P, 8, 512])
            X = sb("X", [P, 8, P])
            XT = sb("XT", [P, 8, P])
            TX = sb("TX", [P, 8, P])
            low0 = sb("low0", [P, SEQ])
            low1 = sb("low1", [P, SEQ])
            psh = sb("psh", [P, 2, SEQ + 1])
            dsh = sb("dsh", [P, SEQ])
            kx = sb("kx", [P, SEQ])
            rx = sb("rx", [P, SEQ])
            t_a = sb("t_a", [P, SEQ])
            t_b = sb("t_b", [P, SEQ])
            t_c = sb("t_c", [P, SEQ])
            t_d = sb("t_d", [P, SEQ])
            t_e = sb("t_e", [P, SEQ])
            t_f = sb("t_f", [P, SEQ])
            zpad = sb("zpad", [P, SEQ + TAPS - 1])
            sgate = dsh
            cv = sb("cv", [P, CT, SEQ])
            ym = sb("ym", [P, CT, SEQ])
            y = sb("y", [P, SEQ])
            ysq = sb("ysq", [P, SEQ])
            G = sb("G", [P, P])
            U = sb("U", [P, P])
            Sp = sb("Sp", [P, 64])
            Sd = sb("Sd", [P, 64])
            emid = sb("emid", [P, 2, TT])
            dec = sb("dec", [P, 2, TT])
            om_ka = sb("om_ka", [P, CT])

        ps = ctx.enter_context(nc.psum_tensor("ps", [P, 8, 512], f32))

        def bank(b, a=0, c=512):
            return ps[:, b, a:c]

        def as2(ap, B):
            return ap.rearrange("p (q b) -> p q b", b=B)

        sems = {}

        def s(name):
            if name not in sems:
                sems[name] = ctx.enter_context(nc.semaphore(name))
            return sems[name]

        block = ctx.enter_context(nc.Block())

        def half_of(t, b, B, side):
            v = t[:, :, :].rearrange("p y (q h b) -> p (y q) h b", h=2, b=B)
            q = P // (2 * B)
            return v[:, 4 * b * q:4 * (b + 1) * q, side, :]

        def half_of_one(t, yy, B, side):
            return t[:, yy, :].rearrange("p (q h b) -> p q h b", h=2, b=B)[:, :, side, :]

        def freed(g, i=0):
            return s(f"gemm_evac{g % 2}"), g // 2 + i

        def evacuated(g, i=0):
            return s(f"gemm_evac{g % 2}"), g // 2 + 1 + i

        NORMS = ["norm_mix0", "norm_ffn0", "norm_mix1", "norm_ffn1", "norm_final"]

        ORDER0 = [("alpha",), ("tok", "v", 0, 0), ("loga",), ("tok", "v", 0, 1), ("tok", "v", 0, 2), ("logb",),
                  ("tok", "v", 0, 3)] + [("tok", "v", 1, t) for t in range(4)]
        ORDER0 += [("k", 0), ("k", 1), ("q", 0), ("q", 1)]
        ORDER0 += [("tok", "sv", 0, 0), ("ktok", 0), ("ktok", 1)] + [("tok", "sv", 0, t) for t in range(1, 4)]
        ORDER0 += [("att", 0)]
        for t in range(4):
            ORDER0 += [("tok", "sv", 1, t), ("kv", 2 * t)] + ([("kv", 2 * t + 1)] if t < 3 else []) + [("ln", t)]
            if t == 0:
                ORDER0 += [("att", 1)]
        for t in range(4):
            ORDER0 += [("tok", "u", 0, t), ("gla_o", t)] + ([("att", t + 2)] if t < 2 else [])
        ORDER0 += [("tok", "u", 1, t) for t in range(4)]
        for t in range(4):
            ORDER0 += [("tok", "g", 0, t), ("sgu", t)]
        for t in range(4):
            ORDER0 += [("tok", "g", 1, t)]
            if t < 3:
                ORDER0 += [("gla_n", t)]
        ORDER0 += [("gla_n", 3)]
        TOK = {"v": (v_tok, 1), "sv": (sv, 5), "u": (u_tok, 7), "g": (g_tok, 9)}

        def quarters(tiles):
            return [("slice", t, q) for t in tiles for q in range(4)]

        def taps_in(c, counts):
            ends = [sum(counts[:i + 1]) for i in range(len(counts))]
            return [[("taps", c, e - n, e)] if n else [] for n, e in zip(counts, ends)]

        ORDER1 = quarters([0]) + quarters([2])[:3] + [("zw", 0), ("slice", 2, 3)] \
            + quarters([4])[:1] + [("za", 0), ("decay_v", 0, 0), ("ksq", 0)] \
            + [("decay", 0, 1), ("decay_v", 0, 1)] + quarters([4])[1:] + [("ks", 0), ("ks_v", 0), ("decay", 0, 2)] \
            + [("decay_v", 0, 2)] + quarters([3]) + [("dyn", 0, 0)] + quarters([14]) \
            + [("dyn", 0, 1), ("bonus", 0)] + quarters([15])
        FILL = {0: [5, 7, 6, 1, 16, 17], 1: [8, 10, 9, 18, 19], 2: [11, 13, 12], 3: [20, 21]}
        SCORE_N = {0: [1] * 6, 1: [1] * 6, 2: [1, 1, 1, 1, 0, 1], 3: [2, 2, 1, 1, 1, 1]}
        LEVEL_N = {0: [1] * 6, 1: [1] * 6, 2: [1, 1, 1, 1, 0, 0], 3: [0] * 6}
        STATE_N = {0: [2, 1] * 4, 1: [1] * 8, 2: [1, 0, 1, 0, 1, 0, 0, 0], 3: [0] * 8}
        LEVEL_TAPS = {0: [5, 5, 2, 4, 1, 2, 3], 1: [5, 5, 2, 2, 1, 1, 3], 2: [5, 5, 2, 2, 1, 1, 3],
                      3: [0, 2, 5, 2, 5, 3, 5]}
        for c in range(CT):
            gaps = quarters(FILL[c])

            def fill(n):
                took = gaps[:n]
                del gaps[:n]
                return took
            left = TAPS - sum(LEVEL_TAPS[c])
            taps = taps_in(c, LEVEL_TAPS[c] + ([4, left - 4, 0, 0] if c == 3 else
                                               [0, left // 2, left - left // 2, 0]))
            mid, end, late = [[] for _ in range(LEVELS)], [[] for _ in range(LEVELS)], []
            if c:
                for i, lv in enumerate((1, 2, 3, 5)):
                    mid[lv] += [("post", c - 1, i)]
                    end[lv] += [("post_v", c - 1, i)]
            if c + 1 < CT:
                mid[1] += [("zw", c + 1)]
                mid[2] += [("za", c + 1)]
                end[2] += [("decay_v", c + 1, 0)]
                mid[3] += [("decay", c + 1, 1), ("ksq", c + 1)]
                end[3] += [("decay_v", c + 1, 1)]
                mid[4] += [("ks", c + 1), ("decay", c + 1, 2)]
                end[4] += [("ks_v", c + 1), ("decay_v", c + 1, 2)]
                end[5] += [("dyn", c + 1, 0)]
                late += [("dyn", c + 1, 1)]
            for i in range(6):
                ORDER1 += [("scores", c, i)] + fill(SCORE_N[c][i])
            ORDER1 += taps[0]
            for lv in range(1, LEVELS):
                ORDER1 += [("tx", c, lv, 0), ("tx", c, lv, 1)] + mid[lv] + fill(LEVEL_N[c][lv - 1])
                ORDER1 += [("dx", c, lv, 0), ("dx", c, lv, 1)] + end[lv] + taps[lv]
            for n in range(TT):
                ORDER1 += [("g", c, n)] + fill(STATE_N[c][2 * n]) + [("u", c, n)] + fill(STATE_N[c][2 * n + 1])
                ORDER1 += [("st", c, n)] + (late if n == 0 else [])
                if c + 1 < CT and n == (3 if c == 2 else 2):
                    ORDER1 += [("bonus", c + 1)]
                ORDER1 += taps[LEVELS + n]
                if c == CT - 1 and n < 3:
                    ORDER1 += [("m", n)]
                if c == CT - 1 and n >= 2:
                    ORDER1 += [("conv_ln", n - 2)]
            ORDER1 += [("ysb", c)]
        ORDER1 += [("post", CT - 1, 0), ("post_v", CT - 1, 0), ("out", 0, 0, 3), ("post", CT - 1, 1), ("conv_ln", 2),
                   ("out", 1, 0, 3), ("post", CT - 1, 2), ("conv_ln", 3), ("m", 3), ("m", 4), ("m", 5), ("m", 6),
                   ("post_v", CT - 1, 2), ("post", CT - 1, 3), ("post_v", CT - 1, 3), ("m", 7)]
        ORDER1 += [("out", 0, 3, 7), ("out", 1, 3, 7), ("out", 0, 7, 8), ("out", 1, 7, 8)]
        M_TILES = [0, 1, 2, 4, 5, 6, 7, 3]

        POS1 = {t: i for i, t in enumerate(ROWS)}
        RKV = ["k", "v", "r"]

        def g1(t):
            return FIRST_TILE[N_MIX1] + POS1[t]

        order, pieces = [], []
        for step in ORDER1:
            order += [step] + pieces[:1]
            pieces = pieces[1:]
            if step[0] == "slice" and step[2] == 3 and POS1[step[1]] % 2 == 1:
                pieces += [("cut", N_MIX1 + POS1[step[1]] // 2 + 2, part) for part in range(4)]
        ORDER1 = order + pieces

        def mu_col(t):
            if t < 2:
                return col("mu_low", t)
            return col("mu_" + RKV[(t - 2) % 3], (t - 2) // 3)

        @block.sync
        def _(sp):
            for n in range(2):
                sp.dma_start(w_raw[:, n, :], weights[n, :, :]).then_inc(s(f"raw_loaded{n}"), 16)
            sp.dma_start(masks_f[:, :], masks_in).then_inc(s("masks_loaded"), 16)
            sp.dma_start(low_w[:, :, :], low_w_in).then_inc(s("low_w_loaded"), 16)
            with sp.Fori(1, CHUNKS // 2) as n:
                for j in range(2):
                    sp.wait_ge(s("lo_done"), 2 * n + (j - 1))
                    sp.dma_start(w_raw[:, j, :], weights[bass.ds(2 * n + j, 1), :, :].rearrange("a p n -> (a p) n"))\
                      .then_inc(s(f"raw_loaded{j}"), 16)
            for k in range(KD):
                sp.wait_ge(s("out_ready"), k + 1)
                sp.dma_start(out[:, k, :], hf[:, k % 3, :]).then_inc(s(f"stored{k % 3}"), 16)
            for r in range(3):
                sp.wait_ge(s(f"stored{r}"), 16 * len(range(r, KD, 3)))

        @block.gpsimd
        def _(pool):
            with pool.Fori(0, CHUNKS // 2) as n:
                for j in range(2):
                    pool.wait_ge(s("hi_done"), 2 * n + (j + 1))
                    pool.tensor_tensor(w_lo[:, j, :], w_raw[:, j, :], w_hi[:, j, :].bitcast(f32), SUB)\
                        .then_inc(s("lo_done"), 1)

        @block.scalar
        def _(act):
            def cut_hi(n, i=None, j=0):
                it = 0 if i is None else i
                act.wait_ge(s(f"raw_loaded{n % 2}"), it * 16 + 16 * (n // 2 + 1))
                if n >= 2:
                    act.wait_ge(s("gemm_done"), it * j + FIRST_TILE[n - 1])
                act.activation(w_hi[:, n % 2, :], w_raw[:, n % 2, :], ACT.Copy).then_inc(s("hi_done"), 1)

            def norm(m):
                act.wait_ge(s("stat_done"), m + 1)
                act.activation(std[:, :], bank(2), ACT.Sqrt, bias=EPS_RMS, scale=1.0 / D).then_inc(s("std_done"), 1)
                if m == 4:
                    return
                for k in range(KD):
                    act.wait_ge(s("hf_done"), 8 * m + k + 1)
                    act.activation(h_hi[:, k, :], hf[:, k % 3, :], ACT.Copy).then_inc(s("h_hi_done"), 1)

            def mlp(layer):
                n0 = N_MLP1 if layer else N_MLP0
                for half in range(2):
                    nu, nd = n0 + 16 * half, n0 + 16 * half + 8
                    r0 = (2 * layer + half) * 16
                    with act.Fori(0, 4) as i:
                        for j in range(2):
                            for t in range(2):
                                g = FIRST_TILE[nu] + 2 * j + t
                                act.wait_ge(s("gemm_done"), i * 4 + (g + 1))
                                act.activation(relu[:, g % 2, :], bank(g % 2), ACT.Relu).then_inc(s("relu_done"), 1)
                            if j == 0:
                                cut_hi_loop(nu + 2, i, 4)
                            else:
                                cut_hi_loop(nu + 3, i, 4)
                    last = layer == 1 and half == 1
                    with act.Fori(0, 3 if last else 4) as i:
                        for j in range(2):
                            cut_hi_loop(nd + 2 + j, i, 2)

            def cut_hi_loop(n, i, per):
                act.wait_ge(s(f"raw_loaded{n % 2}"), i * 16 + 16 * (n // 2 + 1))
                act.wait_ge(s("gemm_done"), i * per + FIRST_TILE[n - 1])
                act.activation(w_hi[:, n % 2, :], w_raw[:, n % 2, :], ACT.Copy).then_inc(s("hi_done"), 1)

            for k in range(KD):
                act.dma_start(x[:, k, :], xT_in[:, k, :]).then_inc(s(f"x_loaded{k}"), 16)
            act.dma_start(cols[:, :], cols_in).then_inc(s("cols_loaded"), 16)
            act.dma_start(mats[:, :, :], mats_in).then_inc(s("mats_loaded"), 16)
            cut_hi(0)
            cut_hi(1)
            act.wait_ge(s("consts_set"), 1)
            act.wait_ge(s("cols_loaded"), 16)
            norm(0)

            act.wait_ge(s("h_ready"), KD)
            act.dma_start(sgu_ln[:, :, :], sgu_ln_in).then_inc(s("sgu_ln_loaded"), 16)
            act.dma_start(sgu_w[:, :, :], sgu_w_in).then_inc(s("sgu_w_loaded"), 16)
            act.dma_start(alpha_w[:, :], alpha_w_in).then_inc(s("alpha_w_loaded"), 16)

            def alpha():
                act.wait_ge(s("gemm_done"), 1)
                act.activation(alrT[:, :], ps[0:16, 0, :], ACT.Copy).then_inc(s("gemm_evac0"), 1)
                cut_hi(2)

            def loga():
                for c in range(2):
                    act.wait_ge(s("z_done"), c + 1)
                    act.activation(zb[:, c, :], bank(2 + c), ACT.Identity, bias=col("b_alpha", c)).then_inc(s("zb_done"), 1)
                    act.wait_ge(s("zb_done"), c + 1)
                    act.activation(zl[:, c, :], zb[:, c, :], ACT.Abs).then_inc(s("zl_done"), 1)
                for c in range(2):
                    act.wait_ge(s("zl_done"), c + 1)
                    act.activation(zl[:, c, :], zl[:, c, :], ACT.Exp, scale=-1.0).then_inc(s("zexp_done"), 1)
                for c in range(2):
                    act.wait_ge(s("zexp_done"), c + 1)
                    act.activation(zl[:, c, :], zl[:, c, :], ACT.Ln, bias=ONE).then_inc(s("zln_done"), 1)

            def logb():
                for c in range(2):
                    act.wait_ge(s("bsum_done"), 2 * c + 1)
                    act.activation(e_neg[:, c, :], bsum[:, c, :], ACT.Exp, scale=-1.0 / 16).then_inc(s("eneg_done"), 1)
                    act.activation(e_pos[:, c, :], bsum[:, c, :], ACT.Exp, scale=1.0 / 16).then_inc(s("epos_done"), 1)
                    act.wait_ge(s("bsum_done"), 2 * c + 2)
                    act.activation(e_end[:, c, :], zb[:, c, :], ACT.Exp, scale=1.0 / 16).then_inc(s("eend_done"), 1)

            def tok(kind, half, t):
                dst, n = TOK[kind]
                n += half
                g = FIRST_TILE[n] + t
                act.wait_ge(s("gemm_done"), g + 1)
                fn = {"v": ACT.Copy, "sv": ACT.Gelu_apprx_tanh, "u": ACT.Gelu_apprx_tanh, "g": ACT.Silu}[kind]
                act.activation(dst[:, t, 256 * half:256 * half + 256], bank(g % 2, 0, 256), fn)\
                   .then_inc(s(f"gemm_evac{g % 2}"), 1)
                if t == 3:
                    cut_hi(n + 2)

            def kq(kind, c):
                if c == 1:
                    cut_hi((3 if kind == "k" else 4) + 2)

            def ktok_(c):
                act.wait_ge(s("ktr_done"), c + 1)
                act.activation(k_tok[:, 2 * c:2 * c + 2, :], bank(4 + c).rearrange("p (t n) -> p t n", n=256),
                               ACT.Copy).then_inc(s("ktok_done"), 1)

            def ln(t):
                act.wait_ge(s("ln_mv_done"), t + 1)
                act.activation(ln_sd[:, t:t + 1], ln_mv[:, t, 1:2], ACT.Sqrt, bias=EPS_LN).then_inc(s("ln_sd_done"), 1)

            def gla_o(t):
                act.wait_ge(s("o_done"), t + 1)
                if t:
                    act.wait_ge(s("oq_done"), t)
                act.activation(o_sb[:, :].rearrange("p (a n) -> p a n", a=2), ps[:, 4:6, 0:256],
                               ACT.Copy).then_inc(s("osb_done"), 1)
                act.wait_ge(s("oms_done"), t + 1)
                act.activation(o_sd[:, t, :], o_ms[:, t, :], ACT.Sqrt, bias=EPS_RMS, scale=1.0 / P).then_inc(s("osd_done"), 1)

            def m_hi(kk, b, count, scale=1.0):
                act.wait_ge(s("mtr_done"), count)
                act.activation(h_hi[:, kk, :], bank(b), ACT.Copy, scale=scale).then_inc(s("m_hi_done"), 1)

            steps = {"alpha": alpha, "loga": loga, "logb": logb, "tok": tok, "k": lambda c: kq("k", c), "q": lambda c: kq("q", c),
                     "ktok": ktok_, "ln": ln, "gla_o": gla_o}
            for name, *a in ORDER0:
                if name in steps:
                    steps[name](*a)
            for i in range(4):
                m_hi(4 + i, 6 + i % 2, i + 1)
            for i in range(4):
                m_hi(i, 2 + i % 2, 5 + i, col("gla_norm", i))
            for n in range(N_OUT0, N_MLP0):
                cut_hi(n + 2)
            norm(1)
            mlp(0)
            norm(2)

            def slice_(t, q):
                if q != 3:
                    return
                g = g1(t)
                act.wait_ge(s("gemm_done"), g + 1)
                if t < 14:
                    i = [u for u in ROWS if u < 14].index(t)
                    act.wait_ge(s("shift_zero"), 1)
                    if i >= 2:
                        act.wait_ge(s("dsh_done"), i - 1)
                    act.activation(psh[:, i % 2, 1:SEQ + 1], bank(g % 2), ACT.Copy).then_inc(s("psh_done"), 1)
                    if t == 0:
                        act.wait_ge(*evacuated(g))
                        act.activation(low0[0:32, :], low0[0:32, :], ACT.Tanh).then_inc(s("low_act"), 1)
                    if t == 1:
                        act.wait_ge(*evacuated(g))
                        act.activation(low1[:, :], low1[:, :], ACT.Sigmoid).then_inc(s("low_act"), 1)
                elif t % 2 == 0:
                    c = (t - 14) // 2
                    act.wait_ge(*evacuated(g - 1))
                    act.activation(sgate[:, :], bank(g % 2), ACT.Sigmoid).then_inc(s(f"gemm_evac{g % 2}"), 1)

            def cut(n, part):
                if part == 0:
                    act.wait_ge(s(f"raw_loaded{n % 2}"), 16 * (n // 2 + 1))
                    act.wait_ge(s("gemm_done"), FIRST_TILE[n - 1])
                at = slice(512 * part, 512 * part + 512)
                i = act.activation(w_hi[:, n % 2, at], w_raw[:, n % 2, at], ACT.Copy)
                if part == 3:
                    i.then_inc(s("hi_done"), 1)

            def zw(c):
                act.wait_ge(s("zw_done"), c + 1)
                if c:
                    act.wait_ge(s("rk_done"), c)
                act.activation(t_a[:, :], bank(6), ACT.Sigmoid, bias=col("w0", c)).then_inc(s("sw_done"), 1)

            def za(c):
                act.wait_ge(s("za_done"), c + 1)
                act.activation(t_e[:, :], bank(6), ACT.Sigmoid, bias=col("a0", c)).then_inc(s("a_done"), 1)

            def decay(c, i):
                if i == 1:
                    act.wait_ge(s("csum_done"), c + 1)
                    act.activation(emid[:, c % 2, :], t_b[:, 63:SEQ:P], ACT.Exp, scale=-EXP_HALF).then_inc(s("emid_done"), 1)
                    act.wait_ge(s("cm_done"), c + 1)
                    act.activation(t_d[:, :], t_c[:, :], ACT.Exp, scale=-EXP_HALF).then_inc(s("ep_done"), 1)
                if i == 2:
                    act.wait_ge(s("ca_done"), c + 1)
                    act.activation(t_b[:, :], t_b[:, :], ACT.Exp, scale=-EXP_HALF).then_inc(s("ea_done"), 1)
                    act.wait_ge(s("ep_done"), c + 1)
                    act.activation(t_c[:, :], t_c[:, :], ACT.Exp, scale=EXP_HALF).then_inc(s("en_done"), 1)

            def ksq(c):
                act.wait_ge(*evacuated(g1(2 + 3 * c)))
                act.activation(t_f[:, :], kx[:, :], ACT.Square, scale=col("k_k", c)).then_inc(s("ksq_done"), 1)

            def ks(c):
                act.wait_ge(s("ksum_done"), c + 1)
                act.activation(t_f[:, :], bank(6), ACT.Sqrt).then_inc(s("knorm_done"), 1)

            def scores(c, i):
                if i == 0:
                    if c:
                        act.wait_ge(s("y_mm"), 4 * c)
                    for t in (X, XT):
                        act.activation(t[:, :, :], mats[:, 0:1, :].broadcast_to([P, 8, P]), ACT.Copy).then_inc(s("x_id"), 1)
                if i == 5:
                    for b, (dst, name) in enumerate(((vtok, "vtok_done"), (btok, "btok_done"), (ktok, "ktok1_done"))):
                        act.wait_ge(s("tok_tr"), 3 * c + b + 1)
                        act.activation(dst[:, :, :], bank((2, 7, 2)[b]).rearrange("p (t n) -> p t n", n=P), ACT.Copy)\
                           .then_inc(s(name), 1)

            def tx(c, lv, b):
                B = 1 << lv
                at = (c * 6 + lv - 1) * 2 + b
                act.wait_ge(s("tx_mm"), at + 1)
                act.activation(half_of(TX, b, B, 0), as2(bank(2 + b, 0, 256), B), ACT.Copy)\
                   .then_inc(s("tx_done"), 1)

            def g_(c, n):
                act.wait_ge(s("g_mm"), 4 * c + n + 1)
                act.activation(G[:, :].rearrange("p (a n) -> p a n", a=2), ps[:, 2:4, 0:64], ACT.Copy).then_inc(s("g_done"), 1)

            def u_(c, n):
                act.wait_ge(s("u_mm"), 4 * c + n + 1)
                act.activation(U[:, :], bank(2, 128, 256), ACT.Copy).then_inc(s("u_done"), 1)

            def ysb(c):
                act.wait_ge(s("y_mm"), 4 * c + 4)
                if c:
                    act.wait_ge(s("ym_done"), c)
                act.activation(y[:, :], bank(7), ACT.Copy).then_inc(s("y_sb"), 1)

            def post(c, i):
                if i == 1:
                    act.wait_ge(s("yc_done"), c + 1)
                    act.activation(ysq[:, :], y[:, :], ACT.Square).then_inc(s("ysq_done"), 1)
                if i == 2:
                    act.wait_ge(s("yvar_mm"), c + 1)
                    act.activation(ysq[:, :], bank(7), ACT.Sqrt, bias=EPS_GN, scale=1.0 / 64).then_inc(s("ysd_done"), 1)
                if i == 3:
                    act.wait_ge(s("yn_done"), c + 1)
                    act.activation(y[:, :], y[:, :], ACT.Identity, bias=col("gn_b", c), scale=col("gn_g", c))\
                       .then_inc(s("yg_done"), 1)

            def conv_ln(i):
                if i == 1:
                    for c in range(CT):
                        act.wait_ge(s("cc_done"), c + 1)
                        act.activation((t_a, t_b, t_d, t_e)[c][:, :], cv[:, c, :], ACT.Square).then_inc(s("csq_done"), 1)
                if i == 2:
                    act.wait_ge(s("cvar_mm"), CT)
                    act.activation(t_c[:, :], bank(5), ACT.Sqrt, bias=EPS_LN, scale=1.0 / 512).then_inc(s("csd_done"), 1)
                if i == 3:
                    for c in range(CT):
                        act.wait_ge(s("cn_done"), c + 1)
                        act.activation(cv[:, c, :], cv[:, c, :], ACT.Silu, bias=col("ln_b", c), scale=col("ln_g", c))\
                           .then_inc(s("cs_done"), 1)

            def m(i):
                k = M_TILES[i]
                act.wait_ge(s("gemm_done"), FIRST_TILE[N_OUT1])
                if k < CT:
                    act.wait_ge(s("ym_done"), k + 1)
                else:
                    act.wait_ge(s("cs_done"), k - CT + 1)
                act.activation(h_hi[:, k, :], ym[:, k, :] if k < CT else cv[:, k - CT, :], ACT.Copy)\
                   .then_inc(s("m_hi_done"), 1)

            steps = {"slice": slice_, "cut": cut, "zw": zw, "za": za, "decay": decay, "ksq": ksq, "ks": ks,
                     "scores": scores, "tx": tx, "g": g_, "u": u_, "ysb": ysb, "post": post, "conv_ln": conv_ln,
                     "m": m}
            for name, *a in ORDER1:
                if name in steps:
                    steps[name](*a)
            for n in range(N_OUT1, N_MLP1):
                cut_hi(n + 2)
            norm(3)
            mlp(1)
            norm(4)

        @block.tensor
        def _(pe):
            def cuts(slot, blk, k, m_hi_, m_lo_):
                a, b = w_hi[:, slot, blk * P:blk * P + P], w_lo[:, slot, blk * P:blk * P + P]
                return ((a, m_hi_), (a, m_lo_), (b, m_hi_))

            def tile(g, slot, t, ks, hi, lo, i=0, per=0, q=None, wait_k=None):
                K = len(ks)
                lot = range(K) if q is None else range(q * K // 4, (q + 1) * K // 4)
                for k in lot:
                    if wait_k is not None:
                        pe.wait_ge(*wait_k(k))
                    for m, (w, r) in enumerate(cuts(slot, t * K + k, k, hi[:, k, :], lo[:, k, :])):
                        if k == 0 and m == 0:
                            if not isinstance(i, int) or g >= 2:
                                pe.wait_ge(s(f"gemm_evac{g % 2}"), per * i + g // 2)
                        mm = pe.matmul(bank(g % 2), w, r, start=(k == 0 and m == 0), stop=(k == K - 1 and m == 2))
                if lot[-1] == K - 1:
                    mm.then_inc(s("gemm_done"), 1)

            def stat(m):
                pe.wait_ge(s("ssq_step"), 9 * (m + 1))
                pe.matmul(bank(2), ONES, ssq[:, :], start=True, stop=True).then_inc(s("stat_done"), 1)

            def mlp(layer):
                n0 = N_MLP1 if layer else N_MLP0
                m = 2 * layer + 1
                for half in range(2):
                    nu, nd = n0 + 16 * half, n0 + 16 * half + 8
                    gu, gd = FIRST_TILE[nu], FIRST_TILE[nd]

                    def up(i, j, wait_k=None):
                        pe.wait_ge(s("lo_done"), 2 * i + (nu + j + 1))
                        for t in range(2):
                            tile(gu + 2 * j + t, (nu + j) % 2, t, range(KD), h_hi, h_lo, i, 2,
                                 wait_k=wait_k if t == 0 else None)
                    if half == 0:
                        up(0, 0, lambda k: (s("h_ready"), 8 * m + k + 1))
                        up(0, 1)
                        start = 1
                    else:
                        start = 0
                    with pe.Fori(start, 4) as i:
                        for j in range(2):
                            up(i, j)
                    pe.wait_ge(*evacuated(gd - 2))
                    pe.wait_ge(*evacuated(gd - 1))
                    with pe.Fori(0, 4) as i:
                        for j in range(2):
                            pe.wait_ge(s("lo_done"), 2 * i + (nd + j + 1))
                            tile(gd + j, (nd + j) % 2, 0, range(HALF_K), f_hi, f_lo, i, 1)

            def out_proj(n0, n1, ready):
                for n in range(n0, n1):
                    pe.wait_ge(s("lo_done"), n + 1)
                    for t in range(2):
                        tile(FIRST_TILE[n] + t, n % 2, t, range(KD), h_hi, h_lo,
                             wait_k=ready if n == n0 and t == 0 else None)

            pe.wait_ge(s("mats_loaded"), 16)
            stat(0)

            def alpha():
                pe.wait_ge(s("lo_done"), 1)
                tile(0, 0, 0, range(KD), h_hi, h_lo, wait_k=lambda k: (s("h_ready"), k + 1))

            def loga():
                pe.wait_ge(s("alpha_w_loaded"), 16)
                pe.wait_ge(s("gemm_evac0"), 1)
                for c in range(2):
                    pe.matmul(bank(2 + c), alpha_w[:, c * P:c * P + P], alrT[:, :], start=True, stop=True)\
                      .then_inc(s("z_done"), 1)

            def tok(kind, half, t):
                n = TOK[kind][1] + half
                if t == 0:
                    pe.wait_ge(s("lo_done"), n + 1)
                g = FIRST_TILE[n] + t
                if g >= 2:
                    pe.wait_ge(*freed(g))
                for k in range(KD):
                    hh, hl = h_hi[:, k, t * P:t * P + P], h_lo[:, k, t * P:t * P + P]
                    wh, wl = w_hi[:, n % 2, k * 256:k * 256 + 256], w_lo[:, n % 2, k * 256:k * 256 + 256]
                    for m, (a, b) in enumerate(((hh, wh), (hh, wl), (hl, wh))):
                        mm = pe.matmul(bank(g % 2, 0, 256), a, b, start=(k == 0 and m == 0), stop=(k == KD - 1 and m == 2))
                mm.then_inc(s("gemm_done"), 1)

            def kq(n, c):
                if c == 0:
                    pe.wait_ge(s("lo_done"), n + 1)
                tile(FIRST_TILE[n] + c, n % 2, c, range(KD), h_hi, h_lo)

            def ktok_(c):
                pe.wait_ge(s("kst_done"), 2)
                for t in range(2):
                    for ch in range(2):
                        tt = 2 * c + t
                        mm = pe.transpose(bank(4 + c, 256 * t + P * ch, 256 * t + P * ch + P),
                                          k_st[:, ch, tt * P:tt * P + P], IDENT)
                mm.then_inc(s("ktr_done"), 1)

            def att_(t):
                pe.wait_ge(*evacuated(FIRST_TILE[5] - 1))
                if t:
                    pe.wait_ge(s("att_done"), t)
                for h in range(4):
                    r = slice(64 * (h % 2), 64 * (h % 2) + 64)
                    at = P * (h // 2)
                    mm = pe.matmul(bank(6 + h % 2, at, at + P), k_dec[r, h // 2, t * P:t * P + P],
                                   q_dec[r, h // 2, t * P:t * P + P], start=True, stop=True)
                mm.then_inc(s("att_mm"), 1)

            def kv(n):
                pe.wait_ge(s("ktok_done"), n // 4 + 1)
                pe.wait_ge(s("eend_done"), 2)
                if n >= 2:
                    pe.wait_ge(s("S_done"), 2 * (n - 1))
                r = slice(64 * (n % 2), 64 * (n % 2) + 64)
                for c in range(2):
                    for h2 in range(2):
                        mm = pe.matmul(ps[64 * h2:64 * h2 + 64, 2 + n % 2, P * c:P * c + P],
                                       k_tok[r, n // 2, c * P + 64 * h2:c * P + 64 * h2 + 64],
                                       v_tok[r, n // 2, (2 * c + h2) * P:(2 * c + h2) * P + P], start=True, stop=True)
                mm.then_inc(s("kv_mm"), 1)

            def gla_o(t):
                pe.wait_ge(s("att_done"), t + 1)
                if t:
                    pe.wait_ge(s("oq_done"), t)
                else:
                    pe.wait_ge(s("ktok_done"), 2)
                if t:
                    pe.wait_ge(s("S_done"), min(4 * t + 2, 14))
                else:
                    pe.wait_ge(s("S_done"), 2)
                for h in range(4):
                    hr = slice(64 * (h % 2), 64 * (h % 2) + 64)
                    at, ah = P * (h // 2), 256 * (h % 2) + P * (h // 2)
                    for e in range(2):
                        n, o = 2 * t + e, ps[64 * e:64 * e + 64, 4 + h % 2, at:at + P]
                        mm = pe.matmul(o, att[:, t % 2, ah + 64 * e:ah + 64 * e + 64], v_tok[:, t, P * h:P * h + P],
                                       start=True, stop=(n == 0))
                        if n:
                            mm = pe.matmul(o, q_dec[hr, h // 2, 64 * n:64 * n + 64], S[hr, n, h // 2, :],
                                           start=False, stop=True)
                mm.then_inc(s("o_done"), 1)

            def sgu(t):
                pe.wait_ge(s("svn_done"), t + 1)
                pe.wait_ge(s("sguw_done"), 1)
                pe.wait_ge(s("S_done"), 14)
                if t >= 2:
                    pe.wait_ge(s("ob_done"), 4 * (t - 1))
                for gg in range(4):
                    mm = pe.matmul(bank(3 - t % 2, P * gg, P * gg + P), sgu_wm[:, gg, :], sv[:, t, P * gg:P * gg + P],
                                   start=True, stop=True)
                mm.then_inc(s("sgu_mm"), 1)

            def m_tr(src, i, b, count):
                for t in range(TT):
                    mm = pe.transpose(bank(b, P * t, P * t + P), src[:, t, P * i:P * i + P], IDENT)
                mm.then_inc(s("mtr_done"), 1)

            steps = {"alpha": alpha, "loga": loga, "tok": tok, "k": lambda c: kq(3, c), "q": lambda c: kq(4, c),
                     "ktok": ktok_, "att": att_, "kv": kv, "gla_o": gla_o, "sgu": sgu}
            for name, *a in ORDER0:
                if name in steps:
                    steps[name](*a)
            for i in range(4):
                pe.wait_ge(s("ob_done"), 16)
                pe.wait_ge(s("att_done"), 4)
                if i >= 2:
                    pe.wait_ge(s("m_lo_done"), i - 1)
                m_tr(u_tok, i, 6 + i % 2, i + 1)
            for i in range(4):
                pe.wait_ge(s("og_done"), 16)
                if i >= 2:
                    pe.wait_ge(s("m_lo_done"), 4 + i - 1)
                m_tr(g_tok, i, 2 + i % 2, 5 + i)
            out_proj(N_OUT0, N_MLP0, lambda k: (s("m_lo_done"), 8))
            stat(1)
            mlp(0)
            stat(2)

            def slice_(t, q):
                g = g1(t)
                at = g - FIRST_TILE[N_MIX1]
                n = N_MIX1 + at // 2
                if at % 2 == 0 and q == 0:
                    pe.wait_ge(s("lo_done"), n + 1)
                tile(g, n % 2, at % 2, range(KD), h_hi, h_lo, q=q,
                     wait_k=(lambda k: (s("h_ready"), 16 + k + 1)) if t == 0 else None)

            def zw(c):
                pe.wait_ge(s("low_w_loaded"), 16)
                pe.wait_ge(s("low_act"), 1)
                if c:
                    pe.wait_ge(s("score_done"), 8 * c)
                pe.matmul(bank(6), low_w[0:32, 0, c * P:c * P + P], low0[0:32, :], start=True, stop=True)\
                  .then_inc(s("zw_done"), 1)

            def za(c):
                pe.wait_ge(s("sw_done"), c + 1)
                pe.matmul(bank(6), low_w[32:64, 0, c * P:c * P + P], low0[32:64, :], start=True, stop=True)\
                  .then_inc(s("za_done"), 1)

            def ks(c):
                pe.wait_ge(s("ksq_done"), c + 1)
                pe.wait_ge(s("a_done"), c + 1)
                pe.matmul(bank(6), BLK, t_f[:, :], start=True, stop=True).then_inc(s("ksum_done"), 1)

            def bonus(c):
                pe.wait_ge(s("rk_done"), c + 1)
                pe.wait_ge(s("knorm_done"), c + 1)
                pe.matmul(bank(6), BLK, rx[:, :], start=True, stop=True).then_inc(s("bonus_mm"), 1)

            def scores(c, i):
                pe.wait_ge(s("rt_done"), c + 1)
                for yy in range(2 * i, 2 * i + 2) if i < 4 else ():
                    n, h2 = yy // 2, yy % 2
                    r = slice(64 * h2, 64 * h2 + 64)
                    if yy >= 2:
                        pe.wait_ge(s("score_done"), 8 * c + yy - 1)
                    elif yy == 1:
                        pe.wait_ge(s("bonus_done"), c + 1)
                    elif c:
                        pe.wait_ge(s("xt_upd"), 12 * c)
                    ar = AR[r, c % 2, n, :, :].rearrange("p a n -> p (a n)")
                    pe.matmul(bank(5 + yy % 2, 0, 256), bT[r, n * P:n * P + P], ar, start=True, stop=True)
                    pe.matmul(bank(5 + yy % 2, 256, 512), kT[r, n * P:n * P + P], ar, start=True, stop=True)\
                      .then_inc(s("score_mm"), 1)
                for yy in range(8) if i == 4 else ():
                    n, h2 = yy // 2, yy % 2
                    r = slice(64 * h2, 64 * h2 + 64)
                    mm = pe.matmul(bank(3 + h2, 64 * n, 64 * n + 64), AR[r, c % 2, n, 0, :],
                                   bT[r, n * P:n * P + P:2], start=True, stop=True)
                if i == 4:
                    mm.then_inc(s("L_mm"), 1)
                if i < 5:
                    return
                if c:
                    pe.wait_ge(s("y_sb"), c)
                for b, src in enumerate((vT, bT, kT)):
                    if b == 2:
                        pe.wait_ge(s("vtok_done"), c + 1)
                    for n in range(TT):
                        mm = pe.transpose(bank((2, 7, 2)[b], P * n, P * n + P), src[:, n * P:n * P + P], IDENT)
                    mm.then_inc(s("tok_tr"), 1)

            def tx(c, lv, b):
                B = 1 << lv
                if lv == 1:
                    pe.wait_ge(s("x_init"), 2 * c + 2)
                    pe.wait_ge(s("ktok1_done"), c + 1)
                else:
                    pe.wait_ge(s("xt_upd"), (6 * c + lv - 2) * 2 + b + 1)
                for yy in range(4 * b, 4 * b + 4):
                    mm = pe.matmul(as2(bank(2 + b, 64 * (yy % 4), 64 * (yy % 4) + 64), B), SC[:, yy, 0:P], half_of_one(X, yy, B, 0),
                                   start=True, stop=True)
                mm.then_inc(s("tx_mm"), 1)

            def dx(c, lv, b):
                B = 1 << lv
                pe.wait_ge(s("tx_done"), (6 * c + lv - 1) * 2 + b + 1)
                for yy in range(4 * b, 4 * b + 4):
                    if lv < LEVELS - 1:
                        pe.matmul(as2(bank(4 + b, 64 * (yy % 4), 64 * (yy % 4) + 64), B), XT[:, yy, :], half_of_one(TX, yy, B, 0),
                                  start=True, stop=True)
                    mm = pe.matmul(as2(bank(4 + b, 256 + 64 * (yy % 4), 320 + 64 * (yy % 4)), B), TX[:, yy, :], half_of_one(XT, yy, B, 1),
                                   start=True, stop=True)
                mm.then_inc(s("dx_mm"), 1)

            def g_(c, n):
                if n == 0:
                    pe.wait_ge(s("xt_upd"), 12 * (c + 1))
                    pe.wait_ge(s("tx_done"), 12 * (c + 1))
                    pe.wait_ge(s("ktok1_done"), c + 1)
                else:
                    pe.wait_ge(s("Sp_done"), 3 * c + n)
                    pe.wait_ge(s("u_done"), 4 * c + n)
                for h2 in range(2):
                    r = slice(64 * h2, 64 * h2 + 64)
                    yy = 2 * n + h2
                    if n:
                        pe.matmul(bank(2 + h2, 0, 64), AR[r, c % 2, n, 0, :], Sp[r, :], start=True, stop=False)
                    mm = pe.matmul(bank(2 + h2, 0, 64), SC[:, yy, 256:384], vtok[:, n, 64 * h2:64 * h2 + 64],
                                   start=(n == 0), stop=True)
                mm.then_inc(s("g_mm"), 1)

            def u_(c, n):
                pe.wait_ge(s("g_done"), 4 * c + n + 1)
                for h2 in range(2):
                    mm = pe.matmul(bank(2, 128 + 64 * h2, 192 + 64 * h2), XT[:, 2 * n + h2, :], G[:, 64 * h2:64 * h2 + 64],
                                   start=True, stop=True)
                mm.then_inc(s("u_mm"), 1)

            def st(c, n):
                pe.wait_ge(s("u_done"), 4 * c + n + 1)
                if c and n == 0:
                    pe.wait_ge(s("ym_done"), c)
                hs = [slice(0, 64), slice(64, P)]
                if n < TT - 1:
                    for r in hs:
                        pe.matmul(ps[r, 2, 256:320], btok[:, n, r], U[:, r], start=True, stop=False)
                        mm = pe.matmul(ps[r, 2, 256:320], ktok[:, n, r], vtok[:, n, r], start=False, stop=True)
                    mm.then_inc(s("s_mm"), 1)
                for h2, r in enumerate(hs):
                    yy = 2 * n + h2
                    o = ps[r, 7, n * P:n * P + P]
                    if n:
                        pe.matmul(o, Sp[r, :], AR[r, c % 2, n, 1, :], start=True, stop=False)
                    pe.matmul(o, U[:, r], SC[:, yy, 128:256], start=(n == 0), stop=False)
                    mm = pe.matmul(o, vtok[:, n, r], SC[:, yy, 384:512], start=False, stop=True)
                mm.then_inc(s("y_mm"), 1)

            def post(c, i):
                if i == 0:
                    pe.wait_ge(s("y_sb"), c + 1)
                    if c < CT - 1:
                        pe.wait_ge(s("btok_done"), c + 2)
                    pe.matmul(bank(7), BLK, y[:, :], start=True, stop=True).then_inc(s("ymean_mm"), 1)
                if i == 2:
                    pe.wait_ge(s("ysq_done"), c + 1)
                    pe.matmul(bank(7), BLK, ysq[:, :], start=True, stop=True).then_inc(s("yvar_mm"), 1)
                if i == 3:
                    pe.wait_ge(s("low_act"), 2)
                    pe.wait_ge(s("ysd_done"), c + 1)
                    pe.matmul(bank(7), low_w[0:96, 1, c * P:c * P + P], low1[0:96, :], start=True, stop=True)\
                      .then_inc(s("gate_mm"), 1)

            def conv_ln(i):
                if i == 0:
                    for c in range(CT):
                        pe.wait_ge(s("tap_done"), TAPS * (c + 1))
                        mm = pe.matmul(bank(4), ONES, cv[:, c, :], start=(c == 0), stop=(c == CT - 1))
                    mm.then_inc(s("cmean_mm"), 1)
                if i == 2:
                    for c in range(CT):
                        pe.wait_ge(s("csq_done"), c + 1)
                        pe.matmul(bank(5), ONES, (t_a, t_b, t_d, t_e)[c][:, :], start=(c == 0), stop=(c == CT - 1))\
                          .then_inc(s("cvar_mm"), 1)

            def out_(t, a, b):
                n, g = N_OUT1, FIRST_TILE[N_OUT1] + t
                if a == 0:
                    pe.wait_ge(s("lo_done"), n + 1)
                    pe.wait_ge(*freed(g))
                for i in range(a, b):
                    k = M_TILES[i]
                    pe.wait_ge(s("m_lo_done"), 8 + i + 1)
                    for m, (w, r) in enumerate(cuts(n % 2, t * KD + k, k, h_hi[:, k, :], h_lo[:, k, :])):
                        mm = pe.matmul(bank(g % 2), w, r, start=(i == 0 and m == 0), stop=(i == KD - 1 and m == 2))
                if b == KD:
                    mm.then_inc(s("gemm_done"), 1)

            steps = {"slice": slice_, "zw": zw, "za": za, "ks": ks, "bonus": bonus, "scores": scores, "tx": tx,
                     "dx": dx, "g": g_, "u": u_, "st": st, "post": post, "conv_ln": conv_ln, "out": out_}
            for name, *a in ORDER1:
                if name in steps:
                    steps[name](*a)
            out_proj(N_OUT1 + 1, N_MLP1, None)
            stat(3)
            mlp(1)
            stat(4)

        @block.vector
        def _(dve):
            tt, stt, ts = dve.tensor_tensor, dve.scalar_tensor_tensor, dve.tensor_scalar
            F = lambda ap: ap.bitcast(f32)

            def norm(m):
                dve.wait_ge(s("std_done"), m + 1)
                dve.reciprocal(rstd[:, :], std[:, :]).then_inc(s("rstd_done"), 1)
                dve.wait_ge(s("rstd_done"), m + 1)
                if m == 4:
                    for k in range(KD):
                        if k >= 3:
                            dve.wait_ge(s(f"stored{k % 3}"), 16 * (k // 3))
                        stt(hf[:, k % 3, :], x[:, k, :], col(NORMS[m], k), rstd[:, :], MUL, MUL).then_inc(s("out_ready"), 1)
                    return

                def lo(k):
                    dve.wait_ge(s("h_hi_done"), 8 * m + k + 1)
                    tt(h_lo[:, k, :], hf[:, k % 3, :], F(h_hi[:, k, :]), SUB).then_inc(s("h_ready"), 1)
                for k in range(KD):
                    if k >= 3:
                        dve.wait_ge(s("h_ready"), 8 * m + k - 2)
                    stt(hf[:, k % 3, :], x[:, k, :], col(NORMS[m], k), rstd[:, :], MUL, MUL).then_inc(s("hf_done"), 1)
                    if k:
                        lo(k - 1)
                lo(KD - 1)

            def residual(n0, m):
                dve.wait_ge(s("gemm_done"), FIRST_TILE[n0] + 1)
                dve.memset(ssq[:, :], 0.0).then_inc(s("ssq_step"), 1)
                for k in range(KD):
                    g = FIRST_TILE[n0] + k
                    dve.wait_ge(s("gemm_done"), g + 1)
                    tt(x[:, k, :], x[:, k, :], bank(g % 2), ADD).then_inc(s(f"gemm_evac{g % 2}"), 1)
                    dve.wait_ge(*evacuated(g))
                    dve.wait_ge(s("ssq_step"), 9 * m + k + 1)
                    tt(xsq[:, :], x[:, k, :], x[:, k, :], MUL).then_inc(s("xsq_done"), 1)
                    dve.wait_ge(s("xsq_done"), 8 * m + k + 1)
                    tt(ssq[:, :], ssq[:, :], xsq[:, :], ADD).then_inc(s("ssq_step"), 1)

            def mlp(layer):
                n0 = N_MLP1 if layer else N_MLP0
                m = 2 * layer + 2
                for half in range(2):
                    nu, nd = n0 + 16 * half, n0 + 16 * half + 8
                    gu, gd = FIRST_TILE[nu], FIRST_TILE[nd]
                    r0 = (2 * layer + half) * 16
                    with dve.Fori(0, 4) as i:
                        for c in range(4):
                            g = gu + c
                            dve.wait_ge(s("relu_done"), 4 * i + (r0 + c + 1))
                            tt(f_hi[:, bass.ds(4 * i + c, 1), :].rearrange("p a n -> p (a n)"), relu[:, g % 2, :],
                               relu[:, g % 2, :], MUL).then_inc(s("fhi_done"), 1)
                            sm, v = evacuated(g - 1)
                            dve.wait_ge(sm, 2 * i + v)
                            tt(f_sq[:, :], relu[:, g % 2, :], relu[:, g % 2, :], MUL).then_inc(s("fsq_done"), 1)
                            dve.wait_ge(s("fhi_done"), 4 * i + (r0 + c + 1))
                            dve.wait_ge(s("fsq_done"), 4 * i + (r0 + c + 1))
                            tt(f_lo[:, bass.ds(4 * i + c, 1), :].rearrange("p a n -> p (a n)"), f_sq[:, :],
                               F(f_hi[:, bass.ds(4 * i + c, 1), :].rearrange("p a n -> p (a n)")), SUB)\
                                .then_inc(s(f"gemm_evac{g % 2}"), 1)
                    if half == 1:
                        dve.memset(ssq[:, :], 0.0).then_inc(s("ssq_step"), 1)
                    with dve.Fori(0, 4) as i:
                        for j in range(2):
                            g = gd + j
                            xk = x[:, bass.ds(2 * i + j, 1), :].rearrange("p a n -> p (a n)")
                            dve.wait_ge(s("gemm_done"), 2 * i + (g + 1))
                            tt(xk, xk, bank(g % 2), ADD).then_inc(s(f"gemm_evac{g % 2}"), 1)
                            if half == 1:
                                sm, v = evacuated(g)
                                dve.wait_ge(sm, i + v)
                                dve.wait_ge(s("ssq_step"), 2 * i + (9 * m + j + 1))
                                tt(xsq[:, :], xk, xk, MUL).then_inc(s("xsq_done"), 1)
                                dve.wait_ge(s("xsq_done"), 2 * i + (8 * m + j + 1))
                                tt(ssq[:, :], ssq[:, :], xsq[:, :], ADD).then_inc(s("ssq_step"), 1)

            for i, v in enumerate((1e-6, 1e-5, 64e-5, 1.0)):
                k_ = dve.memset(eps[:, i:i + 1], v)
            k_.then_inc(s("consts_set"), 1)
            dve.wait_ge(s("masks_loaded"), 16)
            for name, (at, n) in MSRC.items():
                to, m = MCOLS[name]
                dve.tensor_copy(masks[:, to:to + m].rearrange("p (r n) -> p r n", n=n),
                                masks_f[:, at:at + n].rearrange("p (r n) -> p r n", r=1).broadcast_to([P, m // n, n]))\
                   .then_inc(s("mask_bytes"), 1)
            dve.memset(ssq[:, :], 0.0).then_inc(s("ssq_step"), 1)
            for k in range(KD):
                dve.wait_ge(s(f"x_loaded{k}"), 16)
                dve.wait_ge(s("ssq_step"), k + 1)
                tt(xsq[:, :], x[:, k, :], x[:, k, :], MUL).then_inc(s("xsq_done"), 1)
                dve.wait_ge(s("xsq_done"), k + 1)
                tt(ssq[:, :], ssq[:, :], xsq[:, :], ADD).then_inc(s("ssq_step"), 1)
            dve.wait_ge(s("cols_loaded"), 16)
            norm(0)

            dve.wait_ge(s("h_ready"), KD)
            dve.wait_ge(s("mask_bytes"), len(MSRC))
            dve.memset(att[:, :, :], 0.0).then_inc(s("att_zero"), 1)
            dve.memset(sgu_wm[:, :, :], 0.0).then_inc(s("att_zero"), 1)
            dve.wait_ge(s("sgu_w_loaded"), 16)
            dve.wait_ge(s("att_zero"), 2)
            for gg in range(4):
                i = dve.copy_predicated(sgu_wm[:, gg, :], mask("score", 384, 512), sgu_w[:, gg, :])
            i.then_inc(s("sguw_done"), 1)

            def loga():
                for c in range(2):
                    dve.wait_ge(s("zln_done"), c + 1)
                    stt(zb[:, c, :], zb[:, c, :], 0.0, zl[:, c, :], ALU.min, SUB).then_inc(s("la_done"), 1)
                    dve.wait_ge(s("la_done"), c + 1)
                    dve.tensor_tensor_scan(bsum[:, c, :], mask("reset64"), zb[:, c, :], 0.0, MUL, ADD)\
                       .then_inc(s("bsum_done"), 1)
                    dve.wait_ge(s("bsum_done"), 2 * c + 1)
                    b3 = bsum[:, c, :].rearrange("p (n t) -> p n t", t=GLA_CHUNK)
                    tt(zb[:, c, :].rearrange("p (n t) -> p n t", t=GLA_CHUNK),
                       b3[:, :, GLA_CHUNK - 1:GLA_CHUNK].broadcast_to([P, 8, GLA_CHUNK]), b3, SUB)\
                        .then_inc(s("bsum_done"), 1)

            def k_(c):
                g = FIRST_TILE[3] + c
                dve.wait_ge(s("gemm_done"), g + 1)
                dve.wait_ge(s("eend_done"), c + 1)
                tt(k_st[:, c, :], e_end[:, c, :], bank(g % 2), MUL).then_inc(s("kst_done"), 1)
                tt(k_dec[:, c, :], e_neg[:, c, :], bank(g % 2), MUL).then_inc(s(f"gemm_evac{g % 2}"), 1)

            def q_(c):
                g = FIRST_TILE[4] + c
                dve.wait_ge(s("gemm_done"), g + 1)
                dve.wait_ge(s("epos_done"), c + 1)
                stt(q_dec[:, c, :], bank(g % 2), float(64 ** -0.5), e_pos[:, c, :], MUL, MUL)\
                    .then_inc(s(f"gemm_evac{g % 2}"), 1)

            def att_(t):
                dve.wait_ge(s("att_mm"), t + 1)
                if t >= 2:
                    dve.wait_ge(s("o_done"), t - 1)
                dve.copy_predicated(att[:, t % 2, 0:256], mask("gla", 0, 256), bank(6, 0, 256))
                dve.copy_predicated(att[:, t % 2, 256:512], mask("gla", 0, 256), bank(7, 0, 256))\
                   .then_inc(s("att_done"), 1)

            def kv(n):
                dve.wait_ge(s("kv_mm"), n + 1)
                for c in range(2):
                    src = bank(2 + n % 2, P * c, P * c + P)
                    if n == 0:
                        dve.tensor_copy(S[:, 1, c, :], src).then_inc(s("S_done"), 1)
                    else:
                        dve.wait_ge(s("S_done"), 2 * (n - 1) + c + 1)
                        stt(S[:, n + 1, c, :], S[:, n, c, :], e_pos[:, c, 64 * n + 63:64 * n + 64], src, MUL, ADD)\
                            .then_inc(s("S_done"), 1)

            def ln(t):
                g = FIRST_TILE[6] + t
                dve.wait_ge(*evacuated(g))
                dve.wait_ge(*evacuated(FIRST_TILE[5] + t))
                if t == 0:
                    dve.wait_ge(s("sgu_ln_loaded"), 16)
                dve.bn_stats(ln_st[:, t, :], sv[:, t, :]).then_inc(s("ln_st_done"), 1)
                dve.wait_ge(s("ln_st_done"), t + 1)
                dve.bn_aggr(ln_mv[:, t, :], ln_st[:, t, :]).then_inc(s("ln_mv_done"), 1)
                dve.wait_ge(s("ln_sd_done"), t + 1)
                dve.reciprocal(ln_rs[:, t:t + 1], ln_sd[:, t:t + 1]).then_inc(s("ln_rs_done"), 1)
                dve.wait_ge(s("ln_rs_done"), t + 1)
                ts(sv[:, t, :], sv[:, t, :], ln_mv[:, t, 0:1], ln_rs[:, t:t + 1], SUB, MUL).then_inc(s("ln_n"), 1)
                dve.wait_ge(s("ln_n"), 2 * t + 1)
                tt(sv[:, t, :], sv[:, t, :], sgu_ln[:, 0, :], MUL).then_inc(s("ln_n"), 1)
                dve.wait_ge(s("ln_n"), 2 * t + 2)
                tt(sv[:, t, :], sv[:, t, :], sgu_ln[:, 1, :], ADD).then_inc(s("svn_done"), 1)

            def gla_o(t):
                dve.wait_ge(s("osb_done"), t + 1)
                dve.tensor_copy(v_tok[:, t, :], o_sb[:, :]).then_inc(s("ov_done"), 1)
                if t:
                    dve.wait_ge(s("oms_done"), t)
                half = lambda ap: ap.rearrange("p (a n) -> p a n", a=2)
                tt(half(o_sq[:, :]), half(o_sb[:, :]), ps[:, 4:6, 0:256], MUL)\
                    .then_inc(s("oq_done"), 1)
                dve.wait_ge(s("oq_done"), t + 1)
                dve.tensor_reduce(o_ms[:, t, :], o_sq[:, :].rearrange("p (h n) -> p h n", n=P), AX.X, ADD)\
                   .then_inc(s("oms_done"), 1)
                dve.wait_ge(s("osd_done"), t + 1)
                dve.reciprocal(o_rs[:, t, :], o_sd[:, t, :]).then_inc(s("ors_done"), 1)

            def gla_n(t):
                dve.wait_ge(*evacuated(FIRST_TILE[9] + t))
                dve.wait_ge(*evacuated(FIRST_TILE[10] + t))
                dve.wait_ge(s("ors_done"), t + 1)
                dve.wait_ge(s("ov_done"), t + 1)
                for h in range(4):
                    at = slice(P * h, P * h + P)
                    ho = 2 * (h % 2) + h // 2
                    stt(g_tok[:, t, at], v_tok[:, t, P * ho:P * ho + P], o_rs[:, t, ho:ho + 1], g_tok[:, t, at], MUL, MUL)\
                        .then_inc(s("og_done"), 1)

            def sgu(t):
                dve.wait_ge(s("sgu_mm"), t + 1)
                dve.wait_ge(*evacuated(FIRST_TILE[8] + t))
                dve.wait_ge(*evacuated(FIRST_TILE[7] + t))
                for gg in range(4):
                    at = slice(P * gg, P * gg + P)
                    stt(u_tok[:, t, at], bank(3 - t % 2, P * gg, P * gg + P), col("sgu_b", gg), u_tok[:, t, at],
                        ADD, MUL).then_inc(s("ob_done"), 1)

            steps = {"loga": loga, "k": k_, "q": q_, "att": att_, "kv": kv, "ln": ln, "gla_o": gla_o,
                     "gla_n": gla_n, "sgu": sgu}
            for name, *a in ORDER0:
                if name in steps:
                    steps[name](*a)
            for i in range(4):
                dve.wait_ge(s("m_hi_done"), i + 1)
                tt(h_lo[:, 4 + i, :], bank(6 + i % 2), F(h_hi[:, 4 + i, :]), SUB).then_inc(s("m_lo_done"), 1)
            for i in range(4):
                dve.wait_ge(s("m_hi_done"), 5 + i)
                stt(h_lo[:, i, :], bank(2 + i % 2), col("gla_norm", i), F(h_hi[:, i, :]), MUL, SUB)\
                    .then_inc(s("m_lo_done"), 1)
            residual(N_OUT0, 1)
            norm(1)
            mlp(0)
            norm(2)

            dve.wait_ge(s("h_ready"), 3 * KD)
            dve.memset(psh[:, :, 0:1], 0.0).then_inc(s("shift_zero"), 1)
            dve.memset(SC[:, :, :], 0.0).then_inc(s("zeroed"), 1)
            dve.memset(TX[:, :, :], 0.0).then_inc(s("zeroed"), 1)
            dve.memset(zpad[:, 0:TAPS - 1], 0.0).then_inc(s("zeroed"), 1)
            ts(om_ka[:, :], cols[:, COLS["k_a"][0]:COLS["k_a"][0] + 4], -1.0, 1.0, MUL, ADD).then_inc(s("zeroed"), 1)

            def slice_(t, q):
                if q != 3:
                    return
                g = g1(t)
                if t < 14:
                    i = [u for u in ROWS if u < 14].index(t)
                    dve.wait_ge(s("psh_done"), i + 1)
                    dve.wait_ge(*evacuated(g - 1))
                    tt(dsh[:, :], psh[:, i % 2, 0:SEQ], bank(g % 2), SUB).then_inc(s("dsh_done"), 1)
                    if t < 2:
                        dst = (low0, low1)[t]
                    else:
                        c = (t - 2) // 3
                        kind = RKV[(t - 2) % 3]
                        dst = {"k": kx, "v": vT, "r": rx}[kind]
                        if c and kind == "k":
                            dve.wait_ge(s("k2_done"), c)
                        if c and kind == "v":
                            dve.wait_ge(s("bonus_done"), c)
                            dve.wait_ge(s("tok_tr"), 3 * c)
                        if c and kind == "r":
                            dve.wait_ge(s("bonus_mm"), c)
                    dve.wait_ge(s("dsh_done"), i + 1)
                    stt(dst[:, :], dsh[:, :], mu_col(t), bank(g % 2), MUL, ADD).then_inc(s(f"gemm_evac{g % 2}"), 1)
                elif t % 2 == 1:
                    c = (t - 15) // 2
                    dve.wait_ge(*evacuated(g - 1))
                    dve.wait_ge(s("gemm_done"), g + 1)
                    dve.wait_ge(s("zeroed"), 4)
                    if c:
                        dve.wait_ge(s("tap_done"), TAPS * c)
                    tt(zpad[:, TAPS - 1:], sgate[:, :], bank(g % 2), MUL).then_inc(s(f"gemm_evac{g % 2}"), 1)

            def decay(c, i):
                if i == 0:
                    dve.wait_ge(s("sw_done"), c + 1)
                    if c:
                        dve.wait_ge(s("at_done"), c)
                        dve.wait_ge(s("kt_done"), c)
                    dve.tensor_tensor_scan(t_b[:, :], mask("reset128"), t_a[:, :], 0.0, MUL, ADD).then_inc(s("csum_done"), 1)
                    dve.wait_ge(s("csum_done"), c + 1)
                    b3 = t_b[:, :].rearrange("p (n t) -> p n t", t=P)
                    tt(t_c[:, :].rearrange("p (n t) -> p n t", t=P), b3, b3[:, :, 63:64].broadcast_to([P, TT, P]), SUB)\
                        .then_inc(s("cm_done"), 1)
                if i == 1:
                    dve.wait_ge(s("cm_done"), c + 1)
                    dve.wait_ge(s("emid_done"), c + 1)
                    tt(t_b[:, :], t_c[:, :], t_a[:, :], SUB).then_inc(s("ca_done"), 1)
                if i == 2:
                    dve.wait_ge(s("ep_done"), c + 1)
                    tt(dec[:, c % 2, 0:3], t_d[:, 127:SEQ - P:P], emid[:, c % 2, 1:4], MUL).then_inc(s("dec_done"), 1)

            def ks(c):
                dve.wait_ge(s("knorm_done"), c + 1)
                ts(t_f[:, :], t_f[:, :], 1e-12, None, ALU.max).then_inc(s("kn_max"), 1)
                dve.wait_ge(s("kn_max"), c + 1)
                dve.reciprocal(t_f[:, :], t_f[:, :]).then_inc(s("kn_rec"), 1)
                dve.wait_ge(s("kn_rec"), c + 1)
                stt(t_f[:, :], kx[:, :], col("k_k", c), t_f[:, :], MUL, MUL).then_inc(s("kk_done"), 1)

            def dyn(c, part):
                ar = AR[:, c % 2, :, :, :]
                n3 = lambda ap: ap.rearrange("p (n t) -> p n t", t=P)
                if part == 0:
                    dve.wait_ge(s("kk_done"), c + 1)
                    dve.wait_ge(s("ea_done"), c + 1)
                    stt(ar[:, :, 0, :], n3(t_f[:, :]), -1.0, n3(t_b[:, :]), MUL, MUL).then_inc(s("at_done"), 1)
                    dve.wait_ge(s("a_done"), c + 1)
                    dve.wait_ge(s("at_done"), c + 1)
                    tt(t_f[:, :], t_f[:, :], t_e[:, :], MUL).then_inc(s("ab_done"), 1)
                    dve.wait_ge(s("ab_done"), c + 1)
                    dve.wait_ge(s("zeroed"), 4)
                    ts(t_e[:, :], t_e[:, :], col("k_a", c), om_ka[:, c:c + 1], MUL, ADD).then_inc(s("ak_done"), 1)
                    dve.wait_ge(s("en_done"), c + 1)
                    if c:
                        dve.wait_ge(s("tok_tr"), 3 * c)
                        dve.wait_ge(s("L_mm"), c)
                    tt(bT[:, :], t_f[:, :], t_c[:, :], MUL).then_inc(s("bt_done"), 1)
                if part == 1:
                    dve.wait_ge(s("ak_done"), c + 1)
                    tt(t_e[:, :], t_e[:, :], kx[:, :], MUL).then_inc(s("k2_done"), 1)
                    dve.wait_ge(s("k2_done"), c + 1)
                    tt(kT[:, :], t_e[:, :], t_c[:, :], MUL).then_inc(s("kt_done"), 1)
                    dve.wait_ge(*evacuated(g1(4 + 3 * c)))
                    tt(ar[:, :, 1, :], n3(rx[:, :]), n3(t_d[:, :]), MUL).then_inc(s("rt_done"), 1)
                    dve.wait_ge(s("rt_done"), c + 1)
                    stt(rx[:, :], rx[:, :], col("r_k", c), t_e[:, :], MUL, MUL).then_inc(s("rk_done"), 1)

            def bonus(c):
                dve.wait_ge(s("bonus_mm"), c + 1)
                dve.wait_ge(*evacuated(g1(3 + 3 * c)))
                tt(ym[:, c, :], vT[:, :], bank(6), MUL).then_inc(s("bonus_done"), 1)

            def scores(c, i):
                if i == 0:
                    if c:
                        dve.wait_ge(s("y_mm"), 4 * c)
                    dve.wait_ge(s("zeroed"), 4)
                for yy in range(2 * i, 2 * i + 2) if i < 4 else ():
                    dve.wait_ge(s("score_mm"), 8 * c + yy + 1)
                    dve.copy_predicated(SC[:, yy, :], mask("score"), bank(5 + yy % 2)).then_inc(s("score_done"), 1)
                if i != 4:
                    return
                dve.wait_ge(s("L_mm"), c + 1)
                dve.wait_ge(s("x_id"), 2 * c + 2)
                dve.wait_ge(s("score_done"), 8 * c + 8)
                q4 = lambda ap: ap.rearrange("p (y q) -> p y q", q=64)
                for h2 in range(2):
                    xx = X[:, h2:8:2, :].rearrange("p y (q h) -> p y q h", h=2)[:, :, :, 0]
                    dve.copy_predicated(xx, q4(mask("lvlX0", 0, 256)), q4(bank(3 + h2, 0, 256)))
                for b in range(2):
                    lt = SC[:, 4 * b:4 * b + 4, 0:P].rearrange("p y (q h) -> p y q h", h=2)[:, :, :, 1]
                    xt = XT[:, 4 * b:4 * b + 4, :].rearrange("p y (q h) -> p y q h", h=2)[:, :, :, 1]
                    dve.copy_predicated(xt, q4(mask("lvlXT0", 0, 256)), lt).then_inc(s("x_init"), 1)

            def dx(c, lv, b):
                B = 1 << lv
                at = (6 * c + lv - 1) * 2 + b
                dve.wait_ge(s("dx_mm"), at + 1)
                if lv < LEVELS - 1:
                    dve.copy_predicated(half_of(X, b, B, 0), as2(mask(f"lvlX{lv}", 0, 256), B),
                                        as2(bank(4 + b, 0, 256), B))
                dve.copy_predicated(half_of(XT, b, B, 1), as2(mask(f"lvlXT{lv}", 0, 256), B),
                                    as2(bank(4 + b, 256, 512), B)).then_inc(s("xt_upd"), 1)

            def st(c, n):
                if n == TT - 1:
                    return
                at = 3 * c + n
                dve.wait_ge(s("dec_done"), c + 1)
                if n:
                    dve.wait_ge(s("Sp_done"), at)
                    ts(Sd[:, :], Sp[:, :], dec[:, c % 2, n:n + 1], None, MUL).then_inc(s("Sd_done"), 1)
                else:
                    if c:
                        dve.wait_ge(s("Sp_done"), at)
                    dve.memset(Sd[:, :], 0.0).then_inc(s("Sd_done"), 1)
                dve.wait_ge(s("s_mm"), at + 1)
                dve.wait_ge(s("Sd_done"), at + 1)
                if n or c:
                    dve.wait_ge(s("y_mm"), 4 * c + n)
                if n:
                    dve.wait_ge(s("y_mm"), 4 * c + n + 1)
                stt(Sp[:, :], bank(2, 256, 320), dec[:, c % 2, n:n + 1], Sd[:, :], MUL, ADD).then_inc(s("Sp_done"), 1)

            def post(c, i):
                if i == 0:
                    dve.wait_ge(s("ymean_mm"), c + 1)
                    stt(y[:, :], bank(7), -1.0 / 64, y[:, :], MUL, ADD).then_inc(s("yc_done"), 1)
                if i == 2:
                    dve.wait_ge(s("ysd_done"), c + 1)
                    dve.reciprocal(ysq[:, :], ysq[:, :]).then_inc(s("yrs_done"), 1)
                    dve.wait_ge(s("yrs_done"), c + 1)
                    tt(y[:, :], y[:, :], ysq[:, :], MUL).then_inc(s("yn_done"), 1)
                if i == 3:
                    dve.wait_ge(s("yg_done"), c + 1)
                    dve.wait_ge(s("bonus_done"), c + 1)
                    tt(y[:, :], y[:, :], ym[:, c, :], ADD).then_inc(s("yb_done"), 1)
                    dve.wait_ge(s("yb_done"), c + 1)
                    dve.wait_ge(s("gate_mm"), c + 1)
                    tt(ym[:, c, :], y[:, :], bank(7), MUL).then_inc(s("ym_done"), 1)

            def taps(c, a, b):
                for j in range(a, b):
                    if j == 0:
                        dve.wait_ge(*evacuated(g1(15 + 2 * c)))
                        ts(cv[:, c, :], zpad[:, 0:SEQ], col("conv_w", TAPS * c), col("conv_b", c), MUL, ADD)\
                            .then_inc(s("tap_done"), 1)
                    else:
                        dve.wait_ge(s("tap_done"), TAPS * c + j)
                        stt(cv[:, c, :], zpad[:, j:j + SEQ], col("conv_w", TAPS * c + j), cv[:, c, :], MUL, ADD)\
                            .then_inc(s("tap_done"), 1)

            def conv_ln(i):
                if i == 1:
                    dve.wait_ge(s("cmean_mm"), 1)
                    for c in range(CT):
                        stt(cv[:, c, :], bank(4), -1.0 / 512, cv[:, c, :], MUL, ADD).then_inc(s("cc_done"), 1)
                if i == 3:
                    dve.wait_ge(s("csd_done"), 1)
                    dve.reciprocal(t_c[:, :], t_c[:, :]).then_inc(s("crs_done"), 1)
                    dve.wait_ge(s("crs_done"), 1)
                    for c in range(CT):
                        tt(cv[:, c, :], cv[:, c, :], t_c[:, :], MUL).then_inc(s("cn_done"), 1)

            def m(i):
                k = M_TILES[i]
                dve.wait_ge(s("m_hi_done"), KD + i + 1)
                src = ym[:, k, :] if k < CT else cv[:, k - CT, :]
                tt(h_lo[:, k, :], src, F(h_hi[:, k, :]), SUB).then_inc(s("m_lo_done"), 1)

            steps = {"slice": slice_, "decay_v": decay, "ks_v": ks, "dyn": dyn, "bonus": bonus, "scores": scores,
                     "dx": dx, "st": st, "post_v": post, "taps": taps, "conv_ln": conv_ln, "m": m}
            for name, *a in ORDER1:
                if name in steps:
                    steps[name](*a)
            residual(N_OUT1, 3)
            norm(3)
            mlp(1)
            norm(4)


def _both(w, a, b):
    t = np.stack([w[:, a], w[:, b]])
    return t.reshape(2, KD, P, P).transpose(2, 0, 1, 3).reshape(P, 2048)


def _tok(w, c0):
    return w[:, c0:c0 + 256].reshape(KD, P, 256).transpose(1, 0, 2).reshape(P, 2048)


def _down(w, half, d):
    r = HALF_K * P
    return w[half * r:(half + 1) * r, d * P:d * P + P].reshape(HALF_K, P, P).transpose(1, 0, 2).reshape(P, 2048)


def _weights(i):
    R = lambda c: list(range(c, c + P))
    e, o = i["even_w_in"][0], i["odd_w_in"][0]
    out = []
    alr = list(range(1536, 1552)) * 8
    out.append(_both(e, alr, alr))
    out += [_tok(e, 512), _tok(e, 768), _both(e, R(256), R(384)), _both(e, R(0), R(128))]
    out += [_tok(e, 2064), _tok(e, 2320), _tok(e, 1552), _tok(e, 1808), _tok(e, 1024), _tok(e, 1280)]

    def rest(w_out, up, down):
        r = [_both(w_out, R(256 * n), R(256 * n + 128)) for n in range(4)]
        for half in range(2):
            r += [_both(up, R(2048 * half + 256 * n), R(2048 * half + 256 * n + 128)) for n in range(8)]
            r += [_down(down, half, d) for d in range(KD)]
        return r
    out += rest(i["even_w_out"][0], i["w_up"][0], i["w_down"][0])
    xw, xg = list(range(1536, 1600)), list(range(1600, 1696))
    tiles = {0: xw + xw, 1: xg + xg[:32]}
    for c in range(CT):
        tiles[2 + 3 * c] = R(512 + P * c)
        tiles[3 + 3 * c] = R(1024 + P * c)
        tiles[4 + 3 * c] = R(P * c)
        tiles[14 + 2 * c] = R(1696 + 512 + P * c)
        tiles[15 + 2 * c] = R(1696 + P * c)
    out += [_both(o, tiles[ROWS[2 * n]], tiles[ROWS[2 * n + 1]]) for n in range(11)]
    out += rest(i["odd_w_out"][0], i["w_up"][1], i["w_down"][1])
    return np.ascontiguousarray(np.stack(out))


def _cols(i):
    c = np.zeros((P, NCOL), np.float32)

    def put(name, v):
        at, n = COLS[name]
        c[:, at:at + n] = v
    v = lambda a: a.reshape(-1, P).T
    mu = i["rwkv_mu"][0]
    put("norm_mix0", v(i["norm_mix"][0])), put("norm_mix1", v(i["norm_mix"][1]))
    put("norm_ffn0", v(i["norm_ffn"][0])), put("norm_ffn1", v(i["norm_ffn"][1]))
    put("norm_final", v(i["norm_final"]))
    put("b_alpha", v(i["gla_b_alpha"][0])), put("gla_norm", v(i["gla_norm"][0]))
    put("sgu_b", i["sgu_b"][0].T)
    low0, low1 = mu[1536:1600], mu[1600:1696]
    put("mu_low", np.stack([np.concatenate([low0, low0]), np.concatenate([low1, low1[:32]])]).T)
    put("mu_r", v(mu[0:512])), put("mu_k", v(mu[512:1024])), put("mu_v", v(mu[1024:1536]))
    put("w0", v(i["rwkv_w0"][0])), put("a0", v(i["rwkv_a0"][0]))
    put("k_k", v(i["rwkv_k_k"][0])), put("k_a", v(i["rwkv_k_a"][0])), put("r_k", v(i["rwkv_r_k"][0].reshape(-1)))
    put("gn_g", v(i["rwkv_gn_g"][0])), put("gn_b", v(i["rwkv_gn_b"][0]))
    put("conv_b", v(i["conv_b"][0])), put("ln_g", v(i["conv_ln_g"][0])), put("ln_b", v(i["conv_ln_b"][0]))
    put("conv_w", i["conv_w"][0].reshape(TAPS, CT, P).transpose(2, 1, 0).reshape(P, CT * TAPS))
    return c


def _masks():
    p, t = np.arange(P)[:, None], np.arange(P)[None, :]
    m = np.zeros((P, NSRC), np.float32)

    def put(name, v):
        at, n = MSRC[name]
        m[:, at:at + n] = v
    put("gla", (p // 64 == t // 64) & (p <= t))
    put("score", np.concatenate([p < t, p <= t], 1))
    put("reset64", t % GLA_CHUNK != 0)
    put("reset128", t % P != 0)
    for lv in range(LEVELS):
        B = 1 << lv
        pair = (np.arange(64) // B)[None, :]
        put(f"lvlX{lv}", (p // (2 * B) == pair) & (p % (2 * B) >= B))
        put(f"lvlXT{lv}", (p // (2 * B) == pair) & (p % (2 * B) < B))
    return m


def kernel(**inputs):
    import concourse.bacc as bacc
    from concourse.bass_utils import run_bass_kernel_spmd as run

    i = {k: np.asarray(v) for k, v in inputs.items()}
    xT = np.ascontiguousarray(i["x"][0].T.reshape(KD, P, SEQ).transpose(1, 0, 2))
    p, t = np.arange(P)[:, None], np.arange(P)[None, :]
    mats = np.stack([p == t, p == p + 0 * t, p // 64 == t // 64], 1).astype(np.float32)
    sgu_ln = np.ascontiguousarray(np.broadcast_to(np.stack([i["sgu_ln_g"][0], i["sgu_ln_b"][0]]), (P, 2, 512)))
    sgu_w = np.ascontiguousarray(i["sgu_w"][0].transpose(2, 0, 1))
    low_w = np.zeros((P, 2, 512), np.float32)
    low_w[0:32, 0], low_w[32:64, 0], low_w[0:96, 1] = i["rwkv_w2"][0], i["rwkv_a2"][0], i["rwkv_g2"][0]
    arrays = {"xT": xT, "weights": _weights(i), "cols": _cols(i), "mats": mats, "masks": _masks(), "sgu_ln": sgu_ln,
              "sgu_w": sgu_w, "alpha_w": np.ascontiguousarray(i["gla_w_alpha2"][0]), "low_w": low_w}
    nc = bacc.Bacc("TRN2", target_bir_lowering=False, num_devices=1)
    args = [nc.dram_tensor("in_" + k, a.shape, mybir.dt.from_np(a.dtype), kind="ExternalInput").ap()
            for k, a in arrays.items()]
    args.append(nc.dram_tensor("outT", (P, KD, SEQ), mybir.dt.float32, kind="ExternalOutput").ap())
    build(nc, *args)
    r = run(nc, [{"in_" + k: a for k, a in arrays.items()}], core_ids=[0])
    return np.ascontiguousarray(r.results[0]["outT"].transpose(1, 0, 2).reshape(D, SEQ).T).reshape(1, SEQ, D)
```

```python
import concourse.bass as bass
from concourse import mybir
from contextlib import ExitStack

import numpy as np

D = 1024
SEQ = 512
FF = 4 * D
P = 128
KD = D // P
TT = SEQ // P
GLA_CHUNK = 64
RW_CHUNK = 128
TAPS = 31
CT = 4
HALF_K = FF // 2 // P
EXP_HALF = float(np.exp(-0.5))
LEVELS = 7

MIX0 = [1, 4, 4, 2, 2, 4, 4, 4, 4, 4, 4]
MIX1 = [2] * 11
OUTP = [2] * 4
MLPC = ([2] * 8 + [1] * 8) * 2
TILES = MIX0 + OUTP + MLPC + MIX1 + OUTP + MLPC
CHUNKS = len(TILES)
ROWS = [0, 2, 4, 3, 14, 15, 5, 7, 6, 1, 16, 17, 8, 10, 9, 18, 19, 11, 13, 12, 20, 21]
FIRST_TILE = [sum(TILES[:n]) for n in range(CHUNKS + 1)]
N_OUT0 = len(MIX0)
N_MLP0 = N_OUT0 + 4
N_MIX1 = N_MLP0 + 32
N_OUT1 = N_MIX1 + len(MIX1)
N_MLP1 = N_OUT1 + 4

COLS = {}
for _name, _n in (("norm_mix0", 8), ("norm_ffn0", 8), ("norm_mix1", 8), ("norm_ffn1", 8), ("norm_final", 8),
                  ("b_alpha", 2), ("gla_norm", 4), ("sgu_b", 4), ("mu_low", 2), ("mu_k", 4), ("mu_v", 4),
                  ("mu_r", 4), ("w0", 4), ("a0", 4), ("k_k", 4), ("k_a", 4), ("r_k", 4), ("gn_g", 4),
                  ("gn_b", 4), ("conv_b", 4), ("ln_g", 4), ("ln_b", 4), ("conv_w", 4 * TAPS)):
    COLS[_name] = (sum(n for _, n in COLS.values()), _n)
NCOL = sum(n for _, n in COLS.values())

MSRC, MCOLS = {}, {}
for _name, _n, _times in [("gla", 128, 2), ("score", 256, 2), ("reset64", 128, 4), ("reset128", 128, 4)] \
        + [(f"lvl{a}{lv}", 64, 4) for lv in range(LEVELS) for a in ("X", "XT")]:
    MSRC[_name] = (sum(n for _, n in MSRC.values()), _n)
    MCOLS[_name] = (sum(n for _, n in MCOLS.values()), _n * _times)
NSRC = sum(n for _, n in MSRC.values())
NMASK = sum(n for _, n in MCOLS.values())


def build(nc, xT_in, weights, cols_in, mats_in, masks_in, sgu_ln_in, sgu_w_in, alpha_w_in, low_w_in, out):
    f32, f32r, u8 = mybir.dt.float32, mybir.dt.float32r, mybir.dt.uint8
    ALU, ACT, AX = mybir.AluOpType, mybir.ActivationFunctionType, mybir.AxisListType
    MUL, ADD, SUB = ALU.mult, ALU.add, ALU.subtract

    ctx = ExitStack()
    with ctx:
        def tensors(stack):
            def sb(name, shape, dt=f32):
                return stack.enter_context(nc.sbuf_tensor(name, shape, dt))
            return sb

        sb = tensors(ctx)
        x = sb("x", [P, KD, SEQ])
        h_hi = sb("h_hi", [P, KD, SEQ], f32r)
        h_lo = sb("h_lo", [P, KD, SEQ], f32r)
        w_raw = sb("w_raw", [P, 2, 2048])
        w_hi = sb("w_hi", [P, 2, 2048], f32r)
        w_lo = sb("w_lo", [P, 2, 2048], f32r)
        cols = sb("cols", [P, NCOL])
        mats = sb("mats", [P, 3, P])
        masks = sb("masks", [P, NMASK], u8)
        low_w = sb("low_w", [P, 2, 512])
        eps = sb("eps", [P, 4])
        early = sb("early", [P, 5])
        IDENT, ONES, BLK = mats[:, 0, :], mats[:, 1, :], mats[:, 2, :]
        EPS_RMS, EPS_LN, EPS_GN, ONE = (eps[:, i:i + 1] for i in range(4))

        def col(name, i=0):
            at = COLS[name][0] + i
            return cols[:, at:at + 1]

        def mask(name, a=0, b=512):
            at = MCOLS[name][0]
            return masks[:, at + a:at + b]

        with ExitStack() as own:
            sb = tensors(own)
            masks_f = sb("masks_f", [P, NSRC])
            x_sq = sb("x_sq", [P, KD, SEQ])
        with ExitStack() as own:
            sb = tensors(own)
            f_hi = sb("f_hi", [P, HALF_K, SEQ], f32r)
            f_lo = sb("f_lo", [P, HALF_K, SEQ], f32r)
            relu = sb("relu", [P, 2, SEQ])
            f_sq = sb("f_sq", [P, SEQ])
            ssq = sb("ssq", [P, SEQ])
            xsq = sb("xsq", [P, SEQ])
            rms = sb("rms", [P, TT])
            rrms = sb("rrms", [P, TT])
            diag = sb("diag", [P, TT, P])
            hf = sb("hf", [P, 3, SEQ])
        with ExitStack() as own:
            sb = tensors(own)
            sgu_ln = sb("sgu_ln", [P, 2, 512])
            sgu_w = sb("sgu_w", [P, 4, P])
            sgu_wm = sb("sgu_wm", [P, 4, P])
            alpha_w = sb("alpha_w", [16, 256])
            alrT = sb("alrT", [16, SEQ])
            zb = sb("zb", [P, 2, SEQ])
            zl = sb("zl", [P, 2, SEQ])
            bsum = sb("bsum", [P, 2, SEQ])
            e_pos = sb("e_pos", [P, 2, SEQ])
            e_neg = sb("e_neg", [P, 2, SEQ])
            e_end = sb("e_end", [P, 2, SEQ])
            q_dec = sb("q_dec", [P, 2, SEQ])
            k_dec = sb("k_dec", [P, 2, SEQ])
            k_st = sb("k_st", [P, 2, SEQ])
            k_tok = sb("k_tok", [P, TT, 256])
            v_tok = sb("v_tok", [P, TT, 512])
            g_tok = sb("g_tok", [P, TT, 512])
            u_tok = sb("u_tok", [P, TT, 512])
            sv = sb("sv", [P, TT, 512])
            att = sb("att", [P, 2, 512])
            S = sb("S", [P, 8, 2, P])
            o_sb = sb("o_sb", [P, 512])
            o_sq = sb("o_sq", [P, 512])
            o_ms = sb("o_ms", [P, TT, 4])
            o_sd = sb("o_sd", [P, TT, 4])
            o_rs = sb("o_rs", [P, TT, 4])
            ln_st = sb("ln_st", [P, TT, 6])
            ln_mv = sb("ln_mv", [P, TT, 2])
            ln_sd = sb("ln_sd", [P, TT])
            ln_rs = sb("ln_rs", [P, TT])
        with ExitStack() as own:
            sb = tensors(own)
            AR = sb("AR", [P, 2, TT, 2, P])
            bT = sb("bT", [P, SEQ])
            kT = sb("kT", [P, SEQ])
            vT = sb("vT", [P, SEQ])
            vtok = sb("vtok", [P, TT, P])
            btok = sb("btok", [P, TT, P])
            ktok = sb("ktok", [P, TT, P])
            SC = sb("SC", [P, 8, 512])
            X = sb("X", [P, 8, P])
            XT = sb("XT", [P, 8, P])
            TX = sb("TX", [P, 8, P])
            low0 = sb("low0", [P, SEQ])
            low1 = sb("low1", [P, SEQ])
            psh = sb("psh", [P, 2, SEQ + 1])
            dsh = sb("dsh", [P, SEQ])
            kx = sb("kx", [P, SEQ])
            rx = sb("rx", [P, SEQ])
            t_a = sb("t_a", [P, SEQ])
            t_b = sb("t_b", [P, SEQ])
            t_c = sb("t_c", [P, SEQ])
            t_d = sb("t_d", [P, SEQ])
            t_e = sb("t_e", [P, SEQ])
            t_f = sb("t_f", [P, SEQ])
            zpad = sb("zpad", [P, SEQ + TAPS - 1])
            sgate = dsh
            cv = sb("cv", [P, CT, SEQ])
            ym = sb("ym", [P, CT, SEQ])
            y = sb("y", [P, SEQ])
            ysq = sb("ysq", [P, SEQ])
            G = sb("G", [P, P])
            U = sb("U", [P, P])
            Sp = sb("Sp", [P, 64])
            Sd = sb("Sd", [P, 64])
            emid = sb("emid", [P, 2, TT])
            dec = sb("dec", [P, 2, TT])
            om_ka = sb("om_ka", [P, CT])

        ps = ctx.enter_context(nc.psum_tensor("ps", [P, 8, 512], f32))

        def bank(b, a=0, c=512):
            return ps[:, b, a:c]

        def as2(ap, B):
            return ap.rearrange("p (q b) -> p q b", b=B)

        sems = {}

        def s(name):
            if name not in sems:
                sems[name] = ctx.enter_context(nc.semaphore(name))
            return sems[name]

        block = ctx.enter_context(nc.Block())

        def half_of(t, b, B, side):
            v = t[:, :, :].rearrange("p y (q h b) -> p (y q) h b", h=2, b=B)
            q = P // (2 * B)
            return v[:, 4 * b * q:4 * (b + 1) * q, side, :]

        def half_of_one(t, yy, B, side):
            return t[:, yy, :].rearrange("p (q h b) -> p q h b", h=2, b=B)[:, :, side, :]

        SIDE_BY_SIDE = [FIRST_TILE[n] + t for n in (N_MLP0, N_MIX1, N_MLP1) for t in range(2)]

        def gb(g):
            return 4 + g % 2 if g in SIDE_BY_SIDE else g % 2

        def freed(g):
            return s(f"gemm_evac{g % 2}"), g // 2 - (1 if g - 2 in SIDE_BY_SIDE else 0)

        def evacuated(g, i=0):
            return s(f"gemm_evac{g % 2}"), g // 2 + 1 + i

        NORMS = ["norm_mix0", "norm_ffn0", "norm_mix1", "norm_ffn1", "norm_final"]

        ORDER0 = [("alpha",), ("tok", "v", 0, 0), ("loga",), ("tok", "v", 0, 1), ("tok", "v", 0, 2), ("logb",),
                  ("tok", "v", 0, 3)] + [("tok", "v", 1, t) for t in range(4)]
        ORDER0 += [("k", 0), ("k", 1), ("q", 0), ("q", 1)]
        ORDER0 += [("tok", "sv", 0, 0), ("ktok", 0), ("ktok", 1)] + [("tok", "sv", 0, t) for t in range(1, 4)]
        ORDER0 += [("att", 0)]
        for t in range(4):
            ORDER0 += [("tok", "sv", 1, t), ("kv", 2 * t)] + ([("kv", 2 * t + 1)] if t < 3 else []) + [("ln", t)]
            if t == 0:
                ORDER0 += [("att", 1)]
        for t in range(4):
            ORDER0 += [("tok", "u", 0, t), ("gla_o", t)] + ([("att", t + 2)] if t < 2 else [])
        ORDER0 += [("tok", "u", 1, t) for t in range(4)]
        for t in range(4):
            ORDER0 += [("tok", "g", 0, t), ("sgu", t)]
        for t in range(4):
            ORDER0 += [("tok", "g", 1, t), ("utr", t)]
            if t < 3:
                ORDER0 += [("gla_n", t)]
        ORDER0 += [("gla_n", 3)]
        U_BANK, G_BANK = (6, 7, 2, 3), (4, 5, 6, 7)
        TOK = {"v": (v_tok, 1), "sv": (sv, 5), "u": (u_tok, 7), "g": (g_tok, 9)}

        def quarters(tiles):
            return [("slice", t, q) for t in tiles for q in range(4)]

        def taps_in(c, counts):
            ends = [sum(counts[:i + 1]) for i in range(len(counts))]
            return [[("taps", c, e - n, e)] if n else [] for n, e in zip(counts, ends)]

        ORDER1 = [("slice", t, q) for q in range(4) for t in (0, 2)] + quarters([4])[:2] + [("zw", 0)] \
            + quarters([4])[2:3] + [("za", 0), ("decay_v", 0, 0), ("ksq", 0)] \
            + [("decay", 0, 1), ("decay_v", 0, 1)] + quarters([4])[3:] + [("ks", 0), ("ks_v", 0), ("decay", 0, 2)] \
            + [("decay_v", 0, 2)] + quarters([3]) + [("dyn", 0, 0)] + quarters([14]) \
            + [("dyn", 0, 1)] + quarters([15])[:3] + [("bonus", 0), ("slice", 15, 3)]
        FILL = {0: [5, 7, 6, 1, 16, 17], 1: [8, 10, 9, 18, 19], 2: [11, 13, 12], 3: [20, 21]}
        SCORE_N = {0: [1] * 6, 1: [1] * 6, 2: [1, 1, 1, 1, 0, 1], 3: [2, 2, 1, 1, 1, 1]}
        LEVEL_N = {0: [1] * 6, 1: [1] * 6, 2: [1, 1, 1, 1, 0, 0], 3: [0] * 6}
        STATE_N = {0: [2, 1] * 4, 1: [1] * 8, 2: [1, 0, 1, 0, 1, 0, 0, 0], 3: [0] * 8}
        LEVEL_TAPS = {0: [5, 5, 2, 4, 1, 2, 3], 1: [5, 5, 2, 2, 1, 1, 3], 2: [5, 5, 2, 2, 1, 1, 3],
                      3: [1, 3, 5, 2, 5, 4, 5]}
        for c in range(CT):
            gaps = quarters(FILL[c])

            def fill(n):
                took = gaps[:n]
                del gaps[:n]
                return took
            left = TAPS - sum(LEVEL_TAPS[c])
            taps = taps_in(c, LEVEL_TAPS[c] + ([left, 0, 0, 0] if c == 3 else
                                               [0, left // 2, left - left // 2, 0]))
            mid, end, late = [[] for _ in range(LEVELS)], [[] for _ in range(LEVELS)], []
            if c:
                for i, lv in enumerate((1, 2, 3, 6)):
                    mid[lv] += [("post", c - 1, i)]
                    end[lv] += [("post_v", c - 1, i)]
            if c + 1 < CT:
                mid[1] += [("zw", c + 1)]
                mid[2] += [("za", c + 1)]
                end[2] += [("decay_v", c + 1, 0)]
                mid[3] += [("decay", c + 1, 1), ("ksq", c + 1)]
                end[3] += [("decay_v", c + 1, 1)]
                mid[4] += [("ks", c + 1), ("decay", c + 1, 2)]
                end[4] += [("ks_v", c + 1), ("decay_v", c + 1, 2)]
                end[5] += [("dyn", c + 1, 0)]
                late += [("dyn", c + 1, 1)]
            for i in range(6):
                ORDER1 += [("scores", c, i)] + fill(SCORE_N[c][i])
            ORDER1 += taps[0]
            for lv in range(1, LEVELS):
                ORDER1 += [("tx", c, lv, 0), ("tx", c, lv, 1)] + mid[lv] + fill(LEVEL_N[c][lv - 1])
                ORDER1 += [("dx", c, lv, 0), ("dx", c, lv, 1)] + end[lv] + taps[lv]
            for n in range(TT):
                ORDER1 += [("g", c, n)] + fill(STATE_N[c][2 * n]) + [("u", c, n)] + fill(STATE_N[c][2 * n + 1])
                if c == CT - 1 and n == 3:
                    ORDER1 += [("conv_sq",)]
                ORDER1 += [("st", c, n)] + (late if n == 0 else [])
                if c + 1 < CT and n == (3 if c == 2 else 2):
                    ORDER1 += [("bonus", c + 1)]
                ORDER1 += taps[LEVELS + n]
                if c == CT - 1 and n < 3:
                    ORDER1 += [("m", n)]
                if c == CT - 1 and n >= 1:
                    ORDER1 += [("conv_ln", n - 1)]
            ORDER1 += [("ysb", c)]
        ORDER1 += [("conv_ln", 3), ("post", CT - 1, 0), ("post_v", CT - 1, 0), ("conv_ln", 4), ("post", CT - 1, 1),
                   ("out", 0, 0, 3), ("post", CT - 1, 2), ("out", 1, 0, 3), ("conv_ln", 5), ("post_v", CT - 1, 2),
                   ("post", CT - 1, 3), ("post_v", CT - 1, 3), ("m", 3), ("m", 4), ("m", 5), ("m", 6), ("m", 7)]
        ORDER1 += [("out", 0, 3, 7), ("out", 1, 3, 7), ("out", 0, 7, 8), ("out", 1, 7, 8)]
        M_TILES = [0, 1, 2, 4, 5, 6, 7, 3]

        POS1 = {t: i for i, t in enumerate(ROWS)}
        RKV = ["k", "v", "r"]

        def g1(t):
            return FIRST_TILE[N_MIX1] + POS1[t]

        order, held = [], []
        for at, step in enumerate(ORDER1):
            order += [step]
            if step[0] == "slice" and step[2] == 3 and (step[1] < 14 or step[1] % 2):
                held += [("evac_v", step[1])]
            if held and "dx" not in [other[0] for other in ORDER1[at + 1:at + 4]]:
                order += held
                held = []
        ORDER1 = order

        order, pieces = [], []
        for step in ORDER1:
            order += [step] + pieces[:1]
            pieces = pieces[1:]
            if step[0] == "slice" and step[2] == 3 and POS1[step[1]] % 2 == 1:
                pieces += [("cut", N_MIX1 + POS1[step[1]] // 2 + 2, part) for part in range(4)]
        ORDER1 = order + pieces

        def mu_col(t):
            if t < 2:
                return col("mu_low", t)
            return col("mu_" + RKV[(t - 2) % 3], (t - 2) // 3)

        @block.sync
        def _(sp):
            for k in range(0, KD, 2):
                sp.dma_start(x[:, k, :], xT_in[:, k, :]).then_inc(s(f"x_loaded{k}"), 16)
            for n in range(2):
                sp.dma_start(w_raw[:, n, :], weights[n, :, :]).then_inc(s(f"raw_loaded{n}"), 16)
            sp.dma_start(masks_f[:, :], masks_in).then_inc(s("masks_loaded"), 16)
            sp.dma_start(low_w[:, :, :], low_w_in).then_inc(s("low_w_loaded"), 16)
            sp.wait_ge(s("lo_done"), 1)
            sp.dma_start(w_raw[:, 0, :], weights[2, :, :]).then_inc(s("raw_loaded0"), 16)
            sp.wait_ge(s("h_ready"), KD)
            sp.wait_ge(s("mask_bytes"), len(MSRC))
            sp.dma_start(alpha_w[:, :], alpha_w_in).then_inc(s("alpha_w_loaded"), 16)
            sp.dma_start(sgu_ln[:, :, :], sgu_ln_in).then_inc(s("sgu_ln_loaded"), 16)
            sp.dma_start(sgu_w[:, :, :], sgu_w_in).then_inc(s("sgu_w_loaded"), 16)
            sp.wait_ge(s("lo_done"), 2)
            sp.dma_start(w_raw[:, 1, :], weights[3, :, :]).then_inc(s("raw_loaded1"), 16)
            with sp.Fori(2, CHUNKS // 2) as n:
                for j in range(2):
                    sp.wait_ge(s("lo_done"), 2 * n + (j - 1))
                    sp.dma_start(w_raw[:, j, :], weights[bass.ds(2 * n + j, 1), :, :].rearrange("a p n -> (a p) n"))\
                      .then_inc(s(f"raw_loaded{j}"), 16)
            for k in range(KD):
                sp.wait_ge(s("out_ready"), k + 1)
                sp.dma_start(out[:, k, :], x[:, k, :]).then_inc(s("stored"), 16)
            sp.wait_ge(s("stored"), 16 * KD)

        @block.gpsimd
        def _(pool):
            for k in range(3, KD, 2):
                pool.wait_ge(s("sq_odd"), k // 2 + 1)
                if k > 3:
                    pool.wait_ge(s("odd_sum"), k // 2 - 1)
                pool.tensor_tensor(x_sq[:, 1, :], x_sq[:, 1, :], x_sq[:, k, :], ADD).then_inc(s("odd_sum"), 1)
            with pool.Fori(0, CHUNKS // 2) as n:
                for j in range(2):
                    pool.wait_ge(s("hi_done"), 2 * n + (j + 1))
                    pool.tensor_tensor(w_lo[:, j, :], w_raw[:, j, :], w_hi[:, j, :].bitcast(f32), SUB)\
                        .then_inc(s("lo_done"), 1)

        @block.scalar
        def _(act):
            def cut_hi(n, i=None, j=0):
                it = 0 if i is None else i
                act.wait_ge(s(f"raw_loaded{n % 2}"), it * 16 + 16 * (n // 2 + 1))
                if n >= 2:
                    act.wait_ge(s("gemm_done"), it * j + FIRST_TILE[n - 1])
                act.activation(w_hi[:, n % 2, :], w_raw[:, n % 2, :], ACT.Copy).then_inc(s("hi_done"), 1)

            def load_sqrt(m):
                act.activation(early[:, m:m + 1], EPS_RMS, ACT.Sqrt)

            def norm(m):
                act.wait_ge(s("stat_done"), m + 1)
                act.activation(rms[:, :].rearrange("p (t n) -> p t n", n=1), ps[:, 2:6, 0:1], ACT.Sqrt, bias=EPS_RMS, scale=1.0 / D).then_inc(s("std_done"), 1)
                if m == 4:
                    return
                if m == 0:
                    cut_hi(1)
                for k in range(KD):
                    act.wait_ge(s("hf_done"), 8 * m + k + 1)
                    act.activation(h_hi[:, k, :], hf[:, k % 3, :], ACT.Copy).then_inc(s("h_hi_done"), 1)

            def mlp(layer):
                n0 = N_MLP1 if layer else N_MLP0
                for half in range(2):
                    nu, nd = n0 + 16 * half, n0 + 16 * half + 8
                    r0 = (2 * layer + half) * 16
                    if half == 0:
                        for u in range(4):
                            g = FIRST_TILE[nu] + u
                            act.wait_ge(s("gemm_done"), g + 1)
                            if u >= 2:
                                act.wait_ge(s("fhi_done"), r0 + u - 1)
                                act.wait_ge(s("fsq_done"), r0 + u - 1)
                            act.activation(relu[:, g % 2, :], bank(gb(g)), ACT.Relu).then_inc(s("relu_done"), 1)
                            if u % 2:
                                cut_hi(nu + 2 + u // 2)
                    with act.Fori(1 - half, 4) as i:
                        for j in range(2):
                            for t in range(2):
                                g = FIRST_TILE[nu] + 2 * j + t
                                act.wait_ge(s("gemm_done"), i * 4 + (g + 1))
                                act.activation(relu[:, g % 2, :], bank(g % 2), ACT.Relu).then_inc(s("relu_done"), 1)
                            if j == 0:
                                cut_hi_loop(nu + 2, i, 4)
                            else:
                                cut_hi_loop(nu + 3, i, 4)
                    last = layer == 1 and half == 1
                    with act.Fori(0, 3 if last else 4) as i:
                        for j in range(2):
                            cut_hi_loop(nd + 2 + j, i, 2)

            def cut_hi_loop(n, i, per):
                act.wait_ge(s(f"raw_loaded{n % 2}"), i * 16 + 16 * (n // 2 + 1))
                act.wait_ge(s("gemm_done"), i * per + FIRST_TILE[n - 1])
                act.activation(w_hi[:, n % 2, :], w_raw[:, n % 2, :], ACT.Copy).then_inc(s("hi_done"), 1)

            for k in range(1, KD, 2):
                act.dma_start(x[:, k, :], xT_in[:, k, :]).then_inc(s(f"x_loaded{k}"), 16)
            act.dma_start(mats[:, :, :], mats_in).then_inc(s("mats_loaded"), 16)
            act.dma_start(cols[:, :], cols_in).then_inc(s("cols_loaded"), 16)
            act.wait_ge(s("consts_set"), 1)
            load_sqrt(0)
            for k in range(1, KD, 2):
                act.wait_ge(s(f"x_loaded{k}"), 16)
                act.activation(x_sq[:, k, :], x[:, k, :], ACT.Square).then_inc(s("sq_odd"), 1)
            cut_hi(0)
            act.wait_ge(s("cols_loaded"), 16)
            norm(0)


            def alpha():
                act.wait_ge(s("gemm_done"), 1)
                act.activation(alrT[:, :], ps[0:16, 0, :], ACT.Copy).then_inc(s("gemm_evac0"), 1)
                cut_hi(2)

            def loga():
                for c in range(2):
                    act.wait_ge(s("z_done"), c + 1)
                    act.activation(zb[:, c, :], bank(2 + c), ACT.Identity, bias=col("b_alpha", c)).then_inc(s("zb_done"), 1)
                    act.wait_ge(s("zb_done"), c + 1)
                    act.activation(zl[:, c, :], zb[:, c, :], ACT.Abs).then_inc(s("zl_done"), 1)
                for c in range(2):
                    act.wait_ge(s("zl_done"), c + 1)
                    act.activation(zl[:, c, :], zl[:, c, :], ACT.Exp, scale=-1.0).then_inc(s("zexp_done"), 1)
                for c in range(2):
                    act.wait_ge(s("zexp_done"), c + 1)
                    act.activation(zl[:, c, :], zl[:, c, :], ACT.Ln, bias=ONE).then_inc(s("zln_done"), 1)

            def logb():
                for c in range(2):
                    act.wait_ge(s("bsum_done"), 2 * c + 1)
                    act.activation(e_neg[:, c, :], bsum[:, c, :], ACT.Exp, scale=-1.0 / 16).then_inc(s("eneg_done"), 1)
                    act.activation(e_pos[:, c, :], bsum[:, c, :], ACT.Exp, scale=1.0 / 16).then_inc(s("epos_done"), 1)
                    act.wait_ge(s("bsum_done"), 2 * c + 2)
                    act.activation(e_end[:, c, :], zb[:, c, :], ACT.Exp, scale=1.0 / 16).then_inc(s("eend_done"), 1)

            def tok(kind, half, t):
                dst, n = TOK[kind]
                n += half
                g = FIRST_TILE[n] + t
                act.wait_ge(s("gemm_done"), g + 1)
                fn = {"v": ACT.Copy, "sv": ACT.Gelu_apprx_tanh, "u": ACT.Gelu_apprx_tanh, "g": ACT.Silu}[kind]
                act.activation(dst[:, t, 256 * half:256 * half + 256], bank(g % 2, 0, 256), fn)\
                   .then_inc(s(f"gemm_evac{g % 2}"), 1)
                if t == 3:
                    cut_hi(n + 2)

            def kq(kind, c):
                if c == 1:
                    cut_hi((3 if kind == "k" else 4) + 2)

            def ktok_(c):
                act.wait_ge(s("ktr_done"), c + 1)
                act.activation(k_tok[:, 2 * c:2 * c + 2, :], bank(4 + c).rearrange("p (t n) -> p t n", n=256),
                               ACT.Copy).then_inc(s("ktok_done"), 1)

            def ln(t):
                act.wait_ge(s("ln_mv_done"), t + 1)
                act.activation(ln_sd[:, t:t + 1], ln_mv[:, t, 1:2], ACT.Sqrt, bias=EPS_LN).then_inc(s("ln_sd_done"), 1)

            def gla_o(t):
                act.wait_ge(s("o_done"), t + 1)
                if t:
                    act.wait_ge(s("oq_done"), t)
                act.activation(o_sb[:, :].rearrange("p (a n) -> p a n", a=2), ps[:, 4:6, 0:256],
                               ACT.Copy).then_inc(s("osb_done"), 1)
                act.wait_ge(s("oms_done"), t + 1)
                act.activation(o_sd[:, t, :], o_ms[:, t, :], ACT.Sqrt, bias=EPS_RMS, scale=1.0 / P).then_inc(s("osd_done"), 1)

            def m_hi(kk, b, count, scale=1.0):
                act.wait_ge(s("mtr_done"), count)
                act.activation(h_hi[:, kk, :], bank(b), ACT.Copy, scale=scale).then_inc(s("m_hi_done"), 1)

            steps = {"alpha": alpha, "loga": loga, "logb": logb, "tok": tok, "k": lambda c: kq("k", c), "q": lambda c: kq("q", c),
                     "ktok": ktok_, "ln": ln, "gla_o": gla_o}
            for name, *a in ORDER0:
                if name in steps:
                    steps[name](*a)
            act.wait_ge(s("gemm_done"), FIRST_TILE[N_OUT0])
            for i in range(4):
                m_hi(4 + i, U_BANK[i], i + 1)
            for i in range(4):
                m_hi(i, G_BANK[i], 5 + i, col("gla_norm", i))
            for n in range(N_OUT0, N_MLP0):
                if n == N_MLP0 - 1:
                    load_sqrt(1)
                cut_hi(n + 2)
            norm(1)
            mlp(0)
            norm(2)

            def slice_(t, q):
                if q != 3:
                    return
                g = g1(t)
                act.wait_ge(s("gemm_done"), g + 1)
                if t < 14:
                    i = [u for u in ROWS if u < 14].index(t)
                    act.wait_ge(s("zeroed"), 1)
                    if i >= 2:
                        act.wait_ge(s("dsh_done"), i - 1)
                    act.activation(psh[:, i % 2, 1:SEQ + 1], bank(gb(g)), ACT.Copy).then_inc(s("psh_done"), 1)
                    if t == 0:
                        act.wait_ge(*evacuated(g))
                        act.activation(low0[0:32, :], low0[0:32, :], ACT.Tanh).then_inc(s("low_act"), 1)
                    if t == 1:
                        act.wait_ge(*evacuated(g))
                        act.activation(low1[:, :], low1[:, :], ACT.Sigmoid).then_inc(s("low_act"), 1)
                elif t % 2 == 0:
                    c = (t - 14) // 2
                    act.wait_ge(*evacuated(g - 1))
                    act.activation(sgate[:, :], bank(g % 2), ACT.Sigmoid).then_inc(s(f"gemm_evac{g % 2}"), 1)

            def cut(n, part):
                if part == 0:
                    act.wait_ge(s(f"raw_loaded{n % 2}"), 16 * (n // 2 + 1))
                    act.wait_ge(s("gemm_done"), FIRST_TILE[n - 1])
                at = slice(512 * part, 512 * part + 512)
                i = act.activation(w_hi[:, n % 2, at], w_raw[:, n % 2, at], ACT.Copy)
                if part == 3:
                    i.then_inc(s("hi_done"), 1)

            def zw(c):
                act.wait_ge(s("zw_done"), c + 1)
                if c:
                    act.wait_ge(s("rk_done"), c)
                act.activation(t_a[:, :], bank(6), ACT.Sigmoid, bias=col("w0", c)).then_inc(s("sw_done"), 1)

            def za(c):
                act.wait_ge(s("za_done"), c + 1)
                act.activation(t_e[:, :], bank(6), ACT.Sigmoid, bias=col("a0", c)).then_inc(s("a_done"), 1)

            def decay(c, i):
                if i == 1:
                    act.wait_ge(s("cum_step"), 2 * c + 1)
                    act.activation(emid[:, c % 2, :], t_b[:, 63:SEQ:P], ACT.Exp, scale=-EXP_HALF).then_inc(s("emid_done"), 1)
                    act.wait_ge(s("cum_step"), 2 * c + 2)
                    act.activation(t_d[:, :], t_c[:, :], ACT.Exp, scale=-EXP_HALF).then_inc(s("ep_done"), 1)
                if i == 2:
                    act.wait_ge(s("ca_done"), c + 1)
                    act.activation(t_b[:, :], t_b[:, :], ACT.Exp, scale=-EXP_HALF).then_inc(s("ea_done"), 1)
                    act.wait_ge(s("ep_done"), c + 1)
                    act.activation(t_c[:, :], t_c[:, :], ACT.Exp, scale=EXP_HALF).then_inc(s("en_done"), 1)

            def ksq(c):
                act.wait_ge(*evacuated(g1(2 + 3 * c)))
                act.activation(t_f[:, :], kx[:, :], ACT.Square, scale=col("k_k", c)).then_inc(s("ksq_done"), 1)

            def ks(c):
                act.wait_ge(s("ksum_done"), c + 1)
                act.activation(t_f[:, :], bank(6), ACT.Sqrt).then_inc(s("knorm_done"), 1)

            def scores(c, i):
                if i == 0:
                    if c:
                        act.wait_ge(s("y_mm"), 4 * c)
                    for t in (X, XT):
                        act.activation(t[:, :, :], mats[:, 0:1, :].broadcast_to([P, 8, P]), ACT.Copy).then_inc(s("x_id"), 1)
                if i == 5:
                    for b, (dst, name) in enumerate(((vtok, "vtok_done"), (btok, "btok_done"), (ktok, "ktok1_done"))):
                        act.wait_ge(s("tok_tr"), 3 * c + b + 1)
                        act.activation(dst[:, :, :], bank((2, 7, 2)[b]).rearrange("p (t n) -> p t n", n=P), ACT.Copy)\
                           .then_inc(s(name), 1)

            def tx(c, lv, b):
                B = 1 << lv
                at = (c * 6 + lv - 1) * 2 + b
                act.wait_ge(s("tx_mm"), at + 1)
                act.activation(half_of(TX, b, B, 0), as2(bank(2 + b, 0, 256), B), ACT.Copy)\
                   .then_inc(s("tx_done"), 1)

            def g_(c, n):
                act.wait_ge(s("g_mm"), 4 * c + n + 1)
                act.activation(G[:, :].rearrange("p (a n) -> p a n", a=2), ps[:, 2:4, 0:64], ACT.Copy).then_inc(s("g_done"), 1)

            def u_(c, n):
                act.wait_ge(s("u_mm"), 4 * c + n + 1)
                act.activation(U[:, :], bank(2, 128, 256), ACT.Copy).then_inc(s("u_done"), 1)

            def ysb(c):
                act.wait_ge(s("y_mm"), 4 * c + 4)
                if c:
                    act.wait_ge(s("ym_done"), c)
                act.activation(y[:, :], bank(7), ACT.Copy).then_inc(s("y_sb"), 1)

            def post(c, i):
                if i == 1:
                    act.wait_ge(s("yc_done"), c + 1)
                    act.activation(ysq[:, :], y[:, :], ACT.Square).then_inc(s("ysq_done"), 1)
                if i == 2:
                    act.wait_ge(s("yvar_mm"), c + 1)
                    act.activation(ysq[:, :], bank(7), ACT.Sqrt, bias=EPS_GN, scale=1.0 / 64).then_inc(s("ysd_done"), 1)
                if i == 3:
                    act.wait_ge(s("yn_done"), c + 1)
                    act.activation(y[:, :], y[:, :], ACT.Identity, bias=col("gn_b", c), scale=col("gn_g", c))\
                       .then_inc(s("yg_done"), 1)

            def conv_sq():
                for c in range(CT):
                    act.wait_ge(s("cc_done"), c + 1)
                    act.activation((t_a, t_b, t_d, t_e)[c][:, :], cv[:, c, :], ACT.Square).then_inc(s("csq_done"), 1)

            def conv_ln(i):
                if i == 2:
                    act.wait_ge(s("cvar_mm"), CT)
                    act.activation(t_c[:, :], bank(5), ACT.Sqrt, bias=EPS_LN, scale=1.0 / 512).then_inc(s("csd_done"), 1)
                if i == 5:
                    for c in range(CT):
                        act.wait_ge(s("cn_done"), c + 1)
                        act.activation(cv[:, c, :], cv[:, c, :], ACT.Silu, bias=col("ln_b", c), scale=col("ln_g", c))\
                           .then_inc(s("cs_done"), 1)

            def m(i):
                k = M_TILES[i]
                act.wait_ge(s("gemm_done"), FIRST_TILE[N_OUT1])
                if k < CT:
                    act.wait_ge(s("ym_done"), k + 1)
                else:
                    act.wait_ge(s("cs_done"), k - CT + 1)
                act.activation(h_hi[:, k, :], ym[:, k, :] if k < CT else cv[:, k - CT, :], ACT.Copy)\
                   .then_inc(s("m_hi_done"), 1)

            steps = {"slice": slice_, "cut": cut, "zw": zw, "za": za, "decay": decay, "ksq": ksq, "ks": ks,
                     "scores": scores, "tx": tx, "g": g_, "u": u_, "ysb": ysb, "post": post, "conv_ln": conv_ln,
                     "conv_sq": conv_sq, "m": m}
            for name, *a in ORDER1:
                if name in steps:
                    steps[name](*a)
            for n in range(N_OUT1, N_MLP1):
                if n == N_MLP1 - 1:
                    load_sqrt(3)
                cut_hi(n + 2)
            norm(3)
            mlp(1)
            norm(4)

        @block.tensor
        def _(pe):
            def cuts(slot, blk, k, m_hi_, m_lo_):
                a, b = w_hi[:, slot, blk * P:blk * P + P], w_lo[:, slot, blk * P:blk * P + P]
                return ((a, m_hi_), (a, m_lo_), (b, m_hi_))

            def tile(g, slot, t, ks, hi, lo, i=0, per=0, q=None, wait_k=None):
                K = len(ks)
                lot = range(K) if q is None else range(q * K // 4, (q + 1) * K // 4)
                for k in lot:
                    if wait_k is not None:
                        pe.wait_ge(*wait_k(k))
                    for m, (w, r) in enumerate(cuts(slot, t * K + k, k, hi[:, k, :], lo[:, k, :])):
                        if k == 0 and m == 0:
                            if not isinstance(i, int):
                                pe.wait_ge(s(f"gemm_evac{g % 2}"), per * i + g // 2)
                            elif g >= 2:
                                pe.wait_ge(*freed(g))
                        mm = pe.matmul(bank(gb(g) if isinstance(i, int) else g % 2), w, r, start=(k == 0 and m == 0), stop=(k == K - 1 and m == 2))
                if lot[-1] == K - 1:
                    mm.then_inc(s("gemm_done"), 1)

            def token_sums(src, start, stop):
                for t in range(TT):
                    mm = pe.matmul(ps[:, 2 + t, 0:1], src[:, t * P:t * P + P], ONES[:, 0:1], start=start, stop=stop)
                return mm

            def stat(m):
                if m:
                    pe.wait_ge(s("ssq_step"), 8 * m)
                    token_sums(ssq, True, False)
                    pe.wait_ge(s("xsq_done"), 8 * m)
                    token_sums(xsq, False, True).then_inc(s("stat_done"), 1)
                else:
                    pe.wait_ge(s("odd_sum"), 3)
                    token_sums(x_sq[:, 1, :], True, False)
                    pe.wait_ge(s("even_sum"), 7)
                    token_sums(x_sq[:, 0, :], False, True).then_inc(s("stat_done"), 1)
                for t in range(TT):
                    pe.wait_ge(s("diag_done"), 4 * m + t + 1)
                    mm = pe.matmul(bank(6, t * P, t * P + P), ONES, diag[:, t, :], start=True, stop=True)
                mm.then_inc(s("spread_done"), 1)

            def mlp(layer):
                n0 = N_MLP1 if layer else N_MLP0
                m = 2 * layer + 1
                for half in range(2):
                    nu, nd = n0 + 16 * half, n0 + 16 * half + 8
                    gu, gd = FIRST_TILE[nu], FIRST_TILE[nd]

                    def first_up(wait_k):
                        pe.wait_ge(s("lo_done"), nu + 1)
                        for k in range(KD):
                            pe.wait_ge(*wait_k(k))
                            for t in range(2):
                                if k == 0:
                                    pe.wait_ge(*freed(gu + t))
                                for m_, (w, r) in enumerate(cuts(nu % 2, t * KD + k, k, h_hi[:, k, :], h_lo[:, k, :])):
                                    mm = pe.matmul(bank(gb(gu + t)), w, r, start=(k == 0 and m_ == 0),
                                                   stop=(k == KD - 1 and m_ == 2))
                                if k == KD - 1:
                                    mm.then_inc(s("gemm_done"), 1)

                    def up(i, j, wait_k=None):
                        pe.wait_ge(s("lo_done"), 2 * i + (nu + j + 1))
                        for t in range(2):
                            tile(gu + 2 * j + t, (nu + j) % 2, t, range(KD), h_hi, h_lo, i, 2,
                                 wait_k=wait_k if t == 0 else None)
                    if half == 0:
                        first_up(lambda k: (s("h_ready"), 8 * m + k + 1))
                        up(0, 1)
                        start = 1
                    else:
                        start = 0
                    with pe.Fori(start, 4) as i:
                        for j in range(2):
                            up(i, j)
                    relus = 16 * (2 * layer + half) + 16
                    for j in range(2):
                        pe.wait_ge(s("lo_done"), nd + j + 1)
                        pe.wait_ge(s("relu_done"), relus - 1 + j)
                        for k in range(HALF_K):
                            if j == 0:
                                pe.wait_ge(*evacuated(gd - HALF_K + k))
                            for m_, (w, r) in enumerate(cuts((nd + j) % 2, k, k, f_hi[:, k, :], f_lo[:, k, :])):
                                mm = pe.matmul(bank((gd + j) % 2), w, r, start=(k == 0 and m_ == 0),
                                               stop=(k == HALF_K - 1 and m_ == 2))
                        mm.then_inc(s("gemm_done"), 1)
                    with pe.Fori(1, 4) as i:
                        for j in range(2):
                            pe.wait_ge(s("lo_done"), 2 * i + (nd + j + 1))
                            tile(gd + j, (nd + j) % 2, 0, range(HALF_K), f_hi, f_lo, i, 1)

            def out_proj(n0, n1, ready):
                for n in range(n0, n1):
                    pe.wait_ge(s("lo_done"), n + 1)
                    for t in range(2):
                        tile(FIRST_TILE[n] + t, n % 2, t, range(KD), h_hi, h_lo,
                             wait_k=ready if n == n0 and t == 0 else None)

            pe.wait_ge(s("mats_loaded"), 16)
            stat(0)

            def alpha():
                pe.wait_ge(s("lo_done"), 1)
                tile(0, 0, 0, range(KD), h_hi, h_lo, wait_k=lambda k: (s("h_ready"), k + 1))

            def loga():
                pe.wait_ge(s("alpha_w_loaded"), 16)
                pe.wait_ge(s("gemm_evac0"), 1)
                for c in range(2):
                    pe.matmul(bank(2 + c), alpha_w[:, c * P:c * P + P], alrT[:, :], start=True, stop=True)\
                      .then_inc(s("z_done"), 1)

            def tok(kind, half, t):
                n = TOK[kind][1] + half
                if t == 0:
                    pe.wait_ge(s("lo_done"), n + 1)
                g = FIRST_TILE[n] + t
                if g >= 2:
                    pe.wait_ge(*freed(g))
                for k in range(KD):
                    hh, hl = h_hi[:, k, t * P:t * P + P], h_lo[:, k, t * P:t * P + P]
                    wh, wl = w_hi[:, n % 2, k * 256:k * 256 + 256], w_lo[:, n % 2, k * 256:k * 256 + 256]
                    for m, (a, b) in enumerate(((hh, wh), (hh, wl), (hl, wh))):
                        mm = pe.matmul(bank(g % 2, 0, 256), a, b, start=(k == 0 and m == 0), stop=(k == KD - 1 and m == 2))
                mm.then_inc(s("gemm_done"), 1)

            def kq(n, c):
                if c == 0:
                    pe.wait_ge(s("lo_done"), n + 1)
                tile(FIRST_TILE[n] + c, n % 2, c, range(KD), h_hi, h_lo)

            def ktok_(c):
                pe.wait_ge(s("kst_done"), 2)
                for t in range(2):
                    for ch in range(2):
                        tt = 2 * c + t
                        mm = pe.transpose(bank(4 + c, 256 * t + P * ch, 256 * t + P * ch + P),
                                          k_st[:, ch, tt * P:tt * P + P], IDENT)
                mm.then_inc(s("ktr_done"), 1)

            def att_(t):
                pe.wait_ge(*evacuated(FIRST_TILE[5] - 1))
                if t:
                    pe.wait_ge(s("att_done"), t)
                for h in range(4):
                    r = slice(64 * (h % 2), 64 * (h % 2) + 64)
                    at = P * (h // 2)
                    mm = pe.matmul(bank(6 + h % 2, at, at + P), k_dec[r, h // 2, t * P:t * P + P],
                                   q_dec[r, h // 2, t * P:t * P + P], start=True, stop=True)
                mm.then_inc(s("att_mm"), 1)

            def kv(n):
                pe.wait_ge(s("ktok_done"), n // 4 + 1)
                pe.wait_ge(s("eend_done"), 2)
                if n >= 2:
                    pe.wait_ge(s("S_done"), 2 * (n - 1))
                r = slice(64 * (n % 2), 64 * (n % 2) + 64)
                for c in range(2):
                    for h2 in range(2):
                        mm = pe.matmul(ps[64 * h2:64 * h2 + 64, 2 + n % 2, P * c:P * c + P],
                                       k_tok[r, n // 2, c * P + 64 * h2:c * P + 64 * h2 + 64],
                                       v_tok[r, n // 2, (2 * c + h2) * P:(2 * c + h2) * P + P], start=True, stop=True)
                mm.then_inc(s("kv_mm"), 1)

            def gla_o(t):
                pe.wait_ge(s("att_done"), t + 1)
                if t:
                    pe.wait_ge(s("oq_done"), t)
                else:
                    pe.wait_ge(s("ktok_done"), 2)
                if t:
                    pe.wait_ge(s("S_done"), min(4 * t + 2, 14))
                else:
                    pe.wait_ge(s("S_done"), 2)
                for h in range(4):
                    hr = slice(64 * (h % 2), 64 * (h % 2) + 64)
                    at, ah = P * (h // 2), 256 * (h % 2) + P * (h // 2)
                    for e in range(2):
                        n, o = 2 * t + e, ps[64 * e:64 * e + 64, 4 + h % 2, at:at + P]
                        mm = pe.matmul(o, att[:, t % 2, ah + 64 * e:ah + 64 * e + 64], v_tok[:, t, P * h:P * h + P],
                                       start=True, stop=(n == 0))
                        if n:
                            mm = pe.matmul(o, q_dec[hr, h // 2, 64 * n:64 * n + 64], S[hr, n, h // 2, :],
                                           start=False, stop=True)
                mm.then_inc(s("o_done"), 1)

            def sgu(t):
                pe.wait_ge(s("svn_done"), t + 1)
                pe.wait_ge(s("sguw_done"), 1)
                pe.wait_ge(s("S_done"), 14)
                if t >= 2:
                    pe.wait_ge(s("ob_done"), 4 * (t - 1))
                for gg in range(4):
                    mm = pe.matmul(bank(3 - t % 2, P * gg, P * gg + P), sgu_wm[:, gg, :], sv[:, t, P * gg:P * gg + P],
                                   start=True, stop=True)
                mm.then_inc(s("sgu_mm"), 1)

            def m_tr(src, i, b):
                for t in range(TT):
                    mm = pe.transpose(bank(b, P * t, P * t + P), src[:, t, P * i:P * i + P], IDENT)
                mm.then_inc(s("mtr_done"), 1)

            def utr(i):
                pe.wait_ge(s("ob_done"), 16)
                pe.wait_ge(s("att_done"), 4)
                m_tr(u_tok, i, U_BANK[i])

            steps = {"alpha": alpha, "loga": loga, "tok": tok, "k": lambda c: kq(3, c), "q": lambda c: kq(4, c),
                     "ktok": ktok_, "att": att_, "kv": kv, "gla_o": gla_o, "sgu": sgu, "utr": utr}
            for name, *a in ORDER0:
                if name in steps:
                    steps[name](*a)
            for i in range(4):
                pe.wait_ge(s("og_done"), 16)
                if i == 0:
                    pe.wait_ge(s("osb_done"), 4)
                    pe.wait_ge(s("oq_done"), 4)
                if i >= 2:
                    pe.wait_ge(s("m_lo_done"), i - 1)
                m_tr(g_tok, i, G_BANK[i])
            pe.wait_ge(s("lo_done"), N_OUT0 + 1)
            for i, k in enumerate((4, 5, 6, 7, 0, 1, 2, 3)):
                pe.wait_ge(s("m_lo_done"), i + 1)
                for t in range(2):
                    g = FIRST_TILE[N_OUT0] + t
                    if i == 0:
                        pe.wait_ge(*freed(g))
                    for m, (w, r) in enumerate(cuts(N_OUT0 % 2, t * KD + k, k, h_hi[:, k, :], h_lo[:, k, :])):
                        mm = pe.matmul(bank(g % 2), w, r, start=(i == 0 and m == 0), stop=(i == KD - 1 and m == 2))
                    if i == KD - 1:
                        mm.then_inc(s("gemm_done"), 1)
            out_proj(N_OUT0 + 1, N_MLP0, None)
            stat(1)
            mlp(0)
            stat(2)

            def slice_(t, q):
                g = g1(t)
                at = g - FIRST_TILE[N_MIX1]
                n = N_MIX1 + at // 2
                if at % 2 == 0 and q == 0:
                    pe.wait_ge(s("lo_done"), n + 1)
                tile(g, n % 2, at % 2, range(KD), h_hi, h_lo, q=q,
                     wait_k=(lambda k: (s("h_ready"), 16 + k + 1)) if t == 0 else None)

            def zw(c):
                pe.wait_ge(s("low_w_loaded"), 16)
                pe.wait_ge(s("low_act"), 1)
                if c:
                    pe.wait_ge(s("score_done"), 8 * c)
                pe.matmul(bank(6), low_w[0:32, 0, c * P:c * P + P], low0[0:32, :], start=True, stop=True)\
                  .then_inc(s("zw_done"), 1)

            def za(c):
                pe.wait_ge(s("sw_done"), c + 1)
                pe.matmul(bank(6), low_w[32:64, 0, c * P:c * P + P], low0[32:64, :], start=True, stop=True)\
                  .then_inc(s("za_done"), 1)

            def ks(c):
                pe.wait_ge(s("ksq_done"), c + 1)
                pe.wait_ge(s("a_done"), c + 1)
                pe.matmul(bank(6), BLK, t_f[:, :], start=True, stop=True).then_inc(s("ksum_done"), 1)

            def bonus(c):
                pe.wait_ge(s("rk_done"), c + 1)
                pe.wait_ge(s("knorm_done"), c + 1)
                pe.matmul(bank(6), BLK, rx[:, :], start=True, stop=True).then_inc(s("bonus_mm"), 1)

            def scores(c, i):
                pe.wait_ge(s("rt_done"), c + 1)
                for yy in range(2 * i, 2 * i + 2) if i < 4 else ():
                    n, h2 = yy // 2, yy % 2
                    r = slice(64 * h2, 64 * h2 + 64)
                    if yy >= 2:
                        pe.wait_ge(s("score_done"), 8 * c + yy - 1)
                    elif yy == 1:
                        pe.wait_ge(s("bonus_done"), c + 1)
                    elif c:
                        pe.wait_ge(s("xt_upd"), 12 * c)
                    ar = AR[r, c % 2, n, :, :].rearrange("p a n -> p (a n)")
                    pe.matmul(bank(5 + yy % 2, 0, 256), bT[r, n * P:n * P + P], ar, start=True, stop=True)
                    pe.matmul(bank(5 + yy % 2, 256, 512), kT[r, n * P:n * P + P], ar, start=True, stop=True)\
                      .then_inc(s("score_mm"), 1)
                for yy in range(8) if i == 4 else ():
                    n, h2 = yy // 2, yy % 2
                    r = slice(64 * h2, 64 * h2 + 64)
                    mm = pe.matmul(bank(3 + h2, 64 * n, 64 * n + 64), AR[r, c % 2, n, 0, :],
                                   bT[r, n * P:n * P + P:2], start=True, stop=True)
                if i == 4:
                    mm.then_inc(s("L_mm"), 1)
                if i < 5:
                    return
                if c:
                    pe.wait_ge(s("y_sb"), c)
                for b, src in enumerate((vT, bT, kT)):
                    if b == 2:
                        pe.wait_ge(s("vtok_done"), c + 1)
                    for n in range(TT):
                        mm = pe.transpose(bank((2, 7, 2)[b], P * n, P * n + P), src[:, n * P:n * P + P], IDENT)
                    mm.then_inc(s("tok_tr"), 1)

            def tx(c, lv, b):
                B = 1 << lv
                if lv == 1:
                    pe.wait_ge(s("x_init"), 2 * c + 2)
                    pe.wait_ge(s("ktok1_done"), c + 1)
                else:
                    pe.wait_ge(s("xt_upd"), (6 * c + lv - 2) * 2 + b + 1)
                for yy in range(4 * b, 4 * b + 4):
                    mm = pe.matmul(as2(bank(2 + b, 64 * (yy % 4), 64 * (yy % 4) + 64), B), SC[:, yy, 0:P], half_of_one(X, yy, B, 0),
                                   start=True, stop=True)
                mm.then_inc(s("tx_mm"), 1)

            def dx(c, lv, b):
                B = 1 << lv
                pe.wait_ge(s("tx_done"), (6 * c + lv - 1) * 2 + b + 1)
                for yy in range(4 * b, 4 * b + 4):
                    if lv < LEVELS - 1:
                        pe.matmul(as2(bank(4 + b, 64 * (yy % 4), 64 * (yy % 4) + 64), B), XT[:, yy, :], half_of_one(TX, yy, B, 0),
                                  start=True, stop=True)
                    mm = pe.matmul(as2(bank(4 + b, 256 + 64 * (yy % 4), 320 + 64 * (yy % 4)), B), TX[:, yy, :], half_of_one(XT, yy, B, 1),
                                   start=True, stop=True)
                mm.then_inc(s("dx_mm"), 1)

            def g_(c, n):
                if n == 0:
                    pe.wait_ge(s("xt_upd"), 12 * (c + 1))
                    pe.wait_ge(s("tx_done"), 12 * (c + 1))
                    pe.wait_ge(s("ktok1_done"), c + 1)
                else:
                    pe.wait_ge(s("Sp_done"), 3 * c + n)
                    pe.wait_ge(s("u_done"), 4 * c + n)
                for h2 in range(2):
                    r = slice(64 * h2, 64 * h2 + 64)
                    yy = 2 * n + h2
                    if n:
                        pe.matmul(bank(2 + h2, 0, 64), AR[r, c % 2, n, 0, :], Sp[r, :], start=True, stop=False)
                    mm = pe.matmul(bank(2 + h2, 0, 64), SC[:, yy, 256:384], vtok[:, n, 64 * h2:64 * h2 + 64],
                                   start=(n == 0), stop=True)
                mm.then_inc(s("g_mm"), 1)

            def u_(c, n):
                pe.wait_ge(s("g_done"), 4 * c + n + 1)
                for h2 in range(2):
                    mm = pe.matmul(bank(2, 128 + 64 * h2, 192 + 64 * h2), XT[:, 2 * n + h2, :], G[:, 64 * h2:64 * h2 + 64],
                                   start=True, stop=True)
                mm.then_inc(s("u_mm"), 1)

            def st(c, n):
                pe.wait_ge(s("u_done"), 4 * c + n + 1)
                if c and n == 0:
                    pe.wait_ge(s("ym_done"), c)
                hs = [slice(0, 64), slice(64, P)]
                if n < TT - 1:
                    for r in hs:
                        pe.matmul(ps[r, 2, 256:320], btok[:, n, r], U[:, r], start=True, stop=False)
                        mm = pe.matmul(ps[r, 2, 256:320], ktok[:, n, r], vtok[:, n, r], start=False, stop=True)
                    mm.then_inc(s("s_mm"), 1)
                for h2, r in enumerate(hs):
                    yy = 2 * n + h2
                    o = ps[r, 7, n * P:n * P + P]
                    if n:
                        pe.matmul(o, Sp[r, :], AR[r, c % 2, n, 1, :], start=True, stop=False)
                    pe.matmul(o, U[:, r], SC[:, yy, 128:256], start=(n == 0), stop=False)
                    mm = pe.matmul(o, vtok[:, n, r], SC[:, yy, 384:512], start=False, stop=True)
                mm.then_inc(s("y_mm"), 1)

            def post(c, i):
                if i == 0:
                    pe.wait_ge(s("y_sb"), c + 1)
                    if c < CT - 1:
                        pe.wait_ge(s("btok_done"), c + 2)
                    pe.matmul(bank(7), BLK, y[:, :], start=True, stop=True).then_inc(s("ymean_mm"), 1)
                if i == 2:
                    pe.wait_ge(s("ysq_done"), c + 1)
                    pe.matmul(bank(7), BLK, ysq[:, :], start=True, stop=True).then_inc(s("yvar_mm"), 1)
                if i == 3:
                    pe.wait_ge(s("low_act"), 2)
                    pe.wait_ge(s("ysd_done"), c + 1)
                    pe.matmul(bank(7), low_w[0:96, 1, c * P:c * P + P], low1[0:96, :], start=True, stop=True)\
                      .then_inc(s("gate_mm"), 1)

            def conv_ln(i):
                if i == 0:
                    for c in range(CT):
                        pe.wait_ge(s("tap_done"), TAPS * (c + 1))
                        mm = pe.matmul(bank(4), ONES, cv[:, c, :], start=(c == 0), stop=(c == CT - 1))
                    mm.then_inc(s("cmean_mm"), 1)
                if i == 2:
                    for c in range(CT):
                        pe.wait_ge(s("csq_done"), c + 1)
                        pe.matmul(bank(5), ONES, (t_a, t_b, t_d, t_e)[c][:, :], start=(c == 0), stop=(c == CT - 1))\
                          .then_inc(s("cvar_mm"), 1)

            def out_(t, a, b):
                n, g = N_OUT1, FIRST_TILE[N_OUT1] + t
                if a == 0:
                    pe.wait_ge(s("lo_done"), n + 1)
                    pe.wait_ge(*freed(g))
                for i in range(a, b):
                    k = M_TILES[i]
                    pe.wait_ge(s("m_lo_done"), 8 + i + 1)
                    for m, (w, r) in enumerate(cuts(n % 2, t * KD + k, k, h_hi[:, k, :], h_lo[:, k, :])):
                        mm = pe.matmul(bank(g % 2), w, r, start=(i == 0 and m == 0), stop=(i == KD - 1 and m == 2))
                if b == KD:
                    mm.then_inc(s("gemm_done"), 1)

            steps = {"slice": slice_, "zw": zw, "za": za, "ks": ks, "bonus": bonus, "scores": scores, "tx": tx,
                     "dx": dx, "g": g_, "u": u_, "st": st, "post": post, "conv_ln": conv_ln, "out": out_}
            for name, *a in ORDER1:
                if name in steps:
                    steps[name](*a)
            out_proj(N_OUT1 + 1, N_MLP1, None)
            stat(3)
            mlp(1)
            stat(4)

        @block.vector
        def _(dve):
            tt, stt, ts = dve.tensor_tensor, dve.scalar_tensor_tensor, dve.tensor_scalar
            F = lambda ap: ap.bitcast(f32)

            def norm(m):
                dve.wait_ge(s("std_done"), m + 1)
                dve.reciprocal(rrms[:, :], rms[:, :]).then_inc(s("rrms_done"), 1)
                dve.wait_ge(s("rrms_done"), m + 1)
                for t in range(TT):
                    ts(diag[:, t, :], IDENT, rrms[:, t:t + 1], None, MUL).then_inc(s("diag_done"), 1)
                dve.wait_ge(s("spread_done"), m + 1)
                if m == 4:
                    for k in range(KD):
                        stt(x[:, k, :], x[:, k, :], col(NORMS[m], k), bank(6), MUL, MUL).then_inc(s("out_ready"), 1)
                    return

                def lo(k):
                    dve.wait_ge(s("h_hi_done"), 8 * m + k + 1)
                    tt(h_lo[:, k, :], hf[:, k % 3, :], F(h_hi[:, k, :]), SUB).then_inc(s("h_ready"), 1)
                for k in range(KD):
                    if k >= 3:
                        dve.wait_ge(s("h_ready"), 8 * m + k - 2)
                    stt(hf[:, k % 3, :], x[:, k, :], col(NORMS[m], k), bank(6), MUL, MUL).then_inc(s("hf_done"), 1)
                    if k:
                        lo(k - 1)
                lo(KD - 1)

            def residual(n0, m):
                dve.wait_ge(s("gemm_done"), FIRST_TILE[n0] + 1)
                dve.memset(ssq[:, :], 0.0).then_inc(s("ssq_step"), 1)
                for k in range(KD):
                    g = FIRST_TILE[n0] + k
                    dve.wait_ge(s("gemm_done"), g + 1)
                    tt(x[:, k, :], x[:, k, :], bank(g % 2), ADD).then_inc(s(f"gemm_evac{g % 2}"), 1)
                    dve.wait_ge(*evacuated(g))
                    dve.wait_ge(s("ssq_step"), 8 * (m - 1) + k + 1)
                    tt(xsq[:, :], x[:, k, :], x[:, k, :], MUL).then_inc(s("xsq_done"), 1)
                    if k == KD - 1:
                        break
                    dve.wait_ge(s("xsq_done"), 8 * (m - 1) + k + 1)
                    tt(ssq[:, :], ssq[:, :], xsq[:, :], ADD).then_inc(s("ssq_step"), 1)

            def mlp(layer):
                n0 = N_MLP1 if layer else N_MLP0
                m = 2 * layer + 2
                for half in range(2):
                    nu, nd = n0 + 16 * half, n0 + 16 * half + 8
                    gu, gd = FIRST_TILE[nu], FIRST_TILE[nd]
                    r0 = (2 * layer + half) * 16
                    with dve.Fori(0, 4) as i:
                        for c in range(4):
                            g = gu + c
                            dve.wait_ge(s("relu_done"), 4 * i + (r0 + c + 1))
                            tt(f_hi[:, bass.ds(4 * i + c, 1), :].rearrange("p a n -> p (a n)"), relu[:, g % 2, :],
                               relu[:, g % 2, :], MUL).then_inc(s("fhi_done"), 1)
                            sm, v = evacuated(g - 1)
                            dve.wait_ge(sm, 2 * i + v)
                            tt(f_sq[:, :], relu[:, g % 2, :], relu[:, g % 2, :], MUL).then_inc(s("fsq_done"), 1)
                            dve.wait_ge(s("fhi_done"), 4 * i + (r0 + c + 1))
                            dve.wait_ge(s("fsq_done"), 4 * i + (r0 + c + 1))
                            tt(f_lo[:, bass.ds(4 * i + c, 1), :].rearrange("p a n -> p (a n)"), f_sq[:, :],
                               F(f_hi[:, bass.ds(4 * i + c, 1), :].rearrange("p a n -> p (a n)")), SUB)\
                                .then_inc(s(f"gemm_evac{g % 2}"), 1)
                    if half == 1:
                        dve.memset(ssq[:, :], 0.0).then_inc(s("ssq_step"), 1)
                    def add(i, j):
                        g = gd + j
                        xk = x[:, bass.ds(2 * i + j, 1), :].rearrange("p a n -> p (a n)")
                        dve.wait_ge(s("gemm_done"), 2 * i + (g + 1))
                        tt(xk, xk, bank(g % 2), ADD).then_inc(s(f"gemm_evac{g % 2}"), 1)
                        if half == 1:
                            sm, v = evacuated(g)
                            dve.wait_ge(sm, i + v)
                            dve.wait_ge(s("ssq_step"), 2 * i + (8 * (m - 1) + j + 1))
                            tt(xsq[:, :], xk, xk, MUL).then_inc(s("xsq_done"), 1)

                    def add_squares(i, j):
                        dve.wait_ge(s("xsq_done"), 2 * i + (8 * (m - 1) + j + 1))
                        tt(ssq[:, :], ssq[:, :], xsq[:, :], ADD).then_inc(s("ssq_step"), 1)

                    with dve.Fori(0, 3 if half == 1 else 4) as i:
                        for j in range(2):
                            add(i, j)
                            if half == 1:
                                add_squares(i, j)
                    if half == 1:
                        add(3, 0)
                        add_squares(3, 0)
                        add(3, 1)

            for i, v in enumerate((1e-6, 1e-5, 64e-5, 1.0)):
                k_ = dve.memset(eps[:, i:i + 1], v)
            k_.then_inc(s("consts_set"), 1)
            for k in range(0, KD, 2):
                dve.wait_ge(s(f"x_loaded{k}"), 16)
                tt(x_sq[:, k, :], x[:, k, :], x[:, k, :], MUL).then_inc(s("even_sum"), 1)
                if k:
                    dve.wait_ge(s("even_sum"), k)
                    tt(x_sq[:, 0, :], x_sq[:, 0, :], x_sq[:, k, :], ADD).then_inc(s("even_sum"), 1)
            dve.wait_ge(s("cols_loaded"), 16)
            dve.wait_ge(s("stat_done"), 1)
            norm(0)
            dve.wait_ge(s("masks_loaded"), 16)
            for name, (at, n) in MSRC.items():
                to, m = MCOLS[name]
                dve.tensor_copy(masks[:, to:to + m].rearrange("p (r n) -> p r n", n=n),
                                masks_f[:, at:at + n].rearrange("p (r n) -> p r n", r=1).broadcast_to([P, m // n, n]))\
                   .then_inc(s("mask_bytes"), 1)

            dve.wait_ge(s("h_ready"), KD)
            dve.wait_ge(s("mask_bytes"), len(MSRC))
            dve.memset(att[:, :, :], 0.0).then_inc(s("att_zero"), 1)
            dve.memset(sgu_wm[:, :, :], 0.0).then_inc(s("att_zero"), 1)
            dve.wait_ge(s("sgu_w_loaded"), 16)
            dve.wait_ge(s("att_zero"), 2)
            for gg in range(4):
                i = dve.copy_predicated(sgu_wm[:, gg, :], mask("score", 384, 512), sgu_w[:, gg, :])
            i.then_inc(s("sguw_done"), 1)

            def loga():
                for c in range(2):
                    dve.wait_ge(s("zln_done"), c + 1)
                    stt(zb[:, c, :], zb[:, c, :], 0.0, zl[:, c, :], ALU.min, SUB).then_inc(s("la_done"), 1)
                    dve.wait_ge(s("la_done"), c + 1)
                    dve.tensor_tensor_scan(bsum[:, c, :], mask("reset64"), zb[:, c, :], 0.0, MUL, ADD)\
                       .then_inc(s("bsum_done"), 1)
                    dve.wait_ge(s("bsum_done"), 2 * c + 1)
                    b3 = bsum[:, c, :].rearrange("p (n t) -> p n t", t=GLA_CHUNK)
                    tt(zb[:, c, :].rearrange("p (n t) -> p n t", t=GLA_CHUNK),
                       b3[:, :, GLA_CHUNK - 1:GLA_CHUNK].broadcast_to([P, 8, GLA_CHUNK]), b3, SUB)\
                        .then_inc(s("bsum_done"), 1)

            def k_(c):
                g = FIRST_TILE[3] + c
                dve.wait_ge(s("gemm_done"), g + 1)
                dve.wait_ge(s("eend_done"), c + 1)
                tt(k_st[:, c, :], e_end[:, c, :], bank(g % 2), MUL).then_inc(s("kst_done"), 1)
                tt(k_dec[:, c, :], e_neg[:, c, :], bank(g % 2), MUL).then_inc(s(f"gemm_evac{g % 2}"), 1)

            def q_(c):
                g = FIRST_TILE[4] + c
                dve.wait_ge(s("gemm_done"), g + 1)
                dve.wait_ge(s("epos_done"), c + 1)
                stt(q_dec[:, c, :], bank(g % 2), float(64 ** -0.5), e_pos[:, c, :], MUL, MUL)\
                    .then_inc(s(f"gemm_evac{g % 2}"), 1)

            def att_(t):
                dve.wait_ge(s("att_mm"), t + 1)
                if t >= 2:
                    dve.wait_ge(s("o_done"), t - 1)
                dve.copy_predicated(att[:, t % 2, 0:256], mask("gla", 0, 256), bank(6, 0, 256))
                dve.copy_predicated(att[:, t % 2, 256:512], mask("gla", 0, 256), bank(7, 0, 256))\
                   .then_inc(s("att_done"), 1)

            def kv(n):
                dve.wait_ge(s("kv_mm"), n + 1)
                for c in range(2):
                    src = bank(2 + n % 2, P * c, P * c + P)
                    if n == 0:
                        dve.tensor_copy(S[:, 1, c, :], src).then_inc(s("S_done"), 1)
                    else:
                        dve.wait_ge(s("S_done"), 2 * (n - 1) + c + 1)
                        stt(S[:, n + 1, c, :], S[:, n, c, :], e_pos[:, c, 64 * n + 63:64 * n + 64], src, MUL, ADD)\
                            .then_inc(s("S_done"), 1)

            def ln(t):
                g = FIRST_TILE[6] + t
                dve.wait_ge(*evacuated(g))
                dve.wait_ge(*evacuated(FIRST_TILE[5] + t))
                if t == 0:
                    dve.wait_ge(s("sgu_ln_loaded"), 16)
                dve.bn_stats(ln_st[:, t, :], sv[:, t, :]).then_inc(s("ln_st_done"), 1)
                dve.wait_ge(s("ln_st_done"), t + 1)
                dve.bn_aggr(ln_mv[:, t, :], ln_st[:, t, :]).then_inc(s("ln_mv_done"), 1)
                dve.wait_ge(s("ln_sd_done"), t + 1)
                dve.reciprocal(ln_rs[:, t:t + 1], ln_sd[:, t:t + 1]).then_inc(s("ln_rs_done"), 1)
                dve.wait_ge(s("ln_rs_done"), t + 1)
                ts(sv[:, t, :], sv[:, t, :], ln_mv[:, t, 0:1], ln_rs[:, t:t + 1], SUB, MUL).then_inc(s("ln_n"), 1)
                dve.wait_ge(s("ln_n"), 2 * t + 1)
                tt(sv[:, t, :], sv[:, t, :], sgu_ln[:, 0, :], MUL).then_inc(s("ln_n"), 1)
                dve.wait_ge(s("ln_n"), 2 * t + 2)
                tt(sv[:, t, :], sv[:, t, :], sgu_ln[:, 1, :], ADD).then_inc(s("svn_done"), 1)

            def gla_o(t):
                dve.wait_ge(s("osb_done"), t + 1)
                dve.tensor_copy(v_tok[:, t, :], o_sb[:, :]).then_inc(s("ov_done"), 1)
                if t:
                    dve.wait_ge(s("oms_done"), t)
                half = lambda ap: ap.rearrange("p (a n) -> p a n", a=2)
                tt(half(o_sq[:, :]), half(o_sb[:, :]), ps[:, 4:6, 0:256], MUL)\
                    .then_inc(s("oq_done"), 1)
                dve.wait_ge(s("oq_done"), t + 1)
                dve.tensor_reduce(o_ms[:, t, :], o_sq[:, :].rearrange("p (h n) -> p h n", n=P), AX.X, ADD)\
                   .then_inc(s("oms_done"), 1)
                dve.wait_ge(s("osd_done"), t + 1)
                dve.reciprocal(o_rs[:, t, :], o_sd[:, t, :]).then_inc(s("ors_done"), 1)

            def gla_n(t):
                dve.wait_ge(*evacuated(FIRST_TILE[9] + t))
                dve.wait_ge(*evacuated(FIRST_TILE[10] + t))
                dve.wait_ge(s("ors_done"), t + 1)
                dve.wait_ge(s("ov_done"), t + 1)
                for h in range(4):
                    at = slice(P * h, P * h + P)
                    ho = 2 * (h % 2) + h // 2
                    stt(g_tok[:, t, at], v_tok[:, t, P * ho:P * ho + P], o_rs[:, t, ho:ho + 1], g_tok[:, t, at], MUL, MUL)\
                        .then_inc(s("og_done"), 1)

            def sgu(t):
                dve.wait_ge(s("sgu_mm"), t + 1)
                dve.wait_ge(*evacuated(FIRST_TILE[8] + t))
                dve.wait_ge(*evacuated(FIRST_TILE[7] + t))
                for gg in range(4):
                    at = slice(P * gg, P * gg + P)
                    stt(u_tok[:, t, at], bank(3 - t % 2, P * gg, P * gg + P), col("sgu_b", gg), u_tok[:, t, at],
                        ADD, MUL).then_inc(s("ob_done"), 1)

            steps = {"loga": loga, "k": k_, "q": q_, "att": att_, "kv": kv, "ln": ln, "gla_o": gla_o,
                     "gla_n": gla_n, "sgu": sgu}
            for name, *a in ORDER0:
                if name in steps:
                    steps[name](*a)
            for i in range(4):
                dve.wait_ge(s("m_hi_done"), i + 1)
                tt(h_lo[:, 4 + i, :], bank(U_BANK[i]), F(h_hi[:, 4 + i, :]), SUB).then_inc(s("m_lo_done"), 1)
            for i in range(4):
                dve.wait_ge(s("m_hi_done"), 5 + i)
                stt(h_lo[:, i, :], bank(G_BANK[i]), col("gla_norm", i), F(h_hi[:, i, :]), MUL, SUB)\
                    .then_inc(s("m_lo_done"), 1)
            residual(N_OUT0, 1)
            norm(1)
            mlp(0)
            norm(2)

            dve.wait_ge(s("h_ready"), 3 * KD)
            dve.memset(psh[:, :, 0:1], 0.0).then_inc(s("zeroed"), 1)
            dve.memset(SC[:, :, :], 0.0).then_inc(s("zeroed"), 1)
            dve.memset(TX[:, :, :], 0.0).then_inc(s("zeroed"), 1)
            dve.memset(zpad[:, 0:TAPS - 1], 0.0).then_inc(s("zeroed"), 1)
            ts(om_ka[:, :], cols[:, COLS["k_a"][0]:COLS["k_a"][0] + 4], -1.0, 1.0, MUL, ADD).then_inc(s("zeroed"), 1)

            def evac(t):
                g = g1(t)
                if t < 14:
                    i = [u for u in ROWS if u < 14].index(t)
                    dve.wait_ge(s("psh_done"), i + 1)
                    dve.wait_ge(*evacuated(g - 1))
                    tt(dsh[:, :], psh[:, i % 2, 0:SEQ], bank(gb(g)), SUB).then_inc(s("dsh_done"), 1)
                    if t < 2:
                        dst = (low0, low1)[t]
                    else:
                        c = (t - 2) // 3
                        kind = RKV[(t - 2) % 3]
                        dst = {"k": kx, "v": vT, "r": rx}[kind]
                        if c and kind == "k":
                            dve.wait_ge(s("k2_done"), c)
                        if c and kind == "v":
                            dve.wait_ge(s("bonus_done"), c)
                            dve.wait_ge(s("tok_tr"), 3 * c)
                        if c and kind == "r":
                            dve.wait_ge(s("bonus_mm"), c)
                    dve.wait_ge(s("dsh_done"), i + 1)
                    stt(dst[:, :], dsh[:, :], mu_col(t), bank(gb(g)), MUL, ADD).then_inc(s(f"gemm_evac{g % 2}"), 1)
                elif t % 2 == 1:
                    c = (t - 15) // 2
                    dve.wait_ge(*evacuated(g - 1))
                    dve.wait_ge(s("gemm_done"), g + 1)
                    dve.wait_ge(s("zeroed"), 5)
                    if c:
                        dve.wait_ge(s("tap_done"), TAPS * c)
                    tt(zpad[:, TAPS - 1:], sgate[:, :], bank(g % 2), MUL).then_inc(s(f"gemm_evac{g % 2}"), 1)

            def decay(c, i):
                if i == 0:
                    dve.wait_ge(s("sw_done"), c + 1)
                    if c:
                        dve.wait_ge(s("at_done"), c)
                        dve.wait_ge(s("kt_done"), c)
                    dve.tensor_tensor_scan(t_b[:, :], mask("reset128"), t_a[:, :], 0.0, MUL, ADD).then_inc(s("cum_step"), 1)
                    dve.wait_ge(s("cum_step"), 2 * c + 1)
                    b3 = t_b[:, :].rearrange("p (n t) -> p n t", t=P)
                    tt(t_c[:, :].rearrange("p (n t) -> p n t", t=P), b3, b3[:, :, 63:64].broadcast_to([P, TT, P]), SUB)\
                        .then_inc(s("cum_step"), 1)
                if i == 1:
                    dve.wait_ge(s("cum_step"), 2 * c + 2)
                    dve.wait_ge(s("emid_done"), c + 1)
                    tt(t_b[:, :], t_c[:, :], t_a[:, :], SUB).then_inc(s("ca_done"), 1)
                if i == 2:
                    dve.wait_ge(s("ep_done"), c + 1)
                    tt(dec[:, c % 2, 0:3], t_d[:, 127:SEQ - P:P], emid[:, c % 2, 1:4], MUL).then_inc(s("dec_done"), 1)

            def ks(c):
                dve.wait_ge(s("knorm_done"), c + 1)
                ts(t_f[:, :], t_f[:, :], 1e-12, None, ALU.max).then_inc(s("kn_step"), 1)
                dve.wait_ge(s("kn_step"), 2 * c + 1)
                dve.reciprocal(t_f[:, :], t_f[:, :]).then_inc(s("kn_step"), 1)
                dve.wait_ge(s("kn_step"), 2 * c + 2)
                stt(t_f[:, :], kx[:, :], col("k_k", c), t_f[:, :], MUL, MUL).then_inc(s("kk_done"), 1)

            def dyn(c, part):
                ar = AR[:, c % 2, :, :, :]
                n3 = lambda ap: ap.rearrange("p (n t) -> p n t", t=P)
                if part == 0:
                    dve.wait_ge(s("kk_done"), c + 1)
                    dve.wait_ge(s("ea_done"), c + 1)
                    stt(ar[:, :, 0, :], n3(t_f[:, :]), -1.0, n3(t_b[:, :]), MUL, MUL).then_inc(s("at_done"), 1)
                    dve.wait_ge(s("a_done"), c + 1)
                    dve.wait_ge(s("at_done"), c + 1)
                    tt(t_f[:, :], t_f[:, :], t_e[:, :], MUL).then_inc(s("ab_done"), 1)
                    dve.wait_ge(s("ab_done"), c + 1)
                    dve.wait_ge(s("zeroed"), 5)
                    ts(t_e[:, :], t_e[:, :], col("k_a", c), om_ka[:, c:c + 1], MUL, ADD).then_inc(s("ak_done"), 1)
                    dve.wait_ge(s("en_done"), c + 1)
                    if c:
                        dve.wait_ge(s("tok_tr"), 3 * c)
                        dve.wait_ge(s("L_mm"), c)
                    tt(bT[:, :], t_f[:, :], t_c[:, :], MUL).then_inc(s("bt_done"), 1)
                if part == 1:
                    dve.wait_ge(s("ak_done"), c + 1)
                    tt(t_e[:, :], t_e[:, :], kx[:, :], MUL).then_inc(s("k2_done"), 1)
                    dve.wait_ge(s("k2_done"), c + 1)
                    tt(kT[:, :], t_e[:, :], t_c[:, :], MUL).then_inc(s("kt_done"), 1)
                    dve.wait_ge(*evacuated(g1(4 + 3 * c)))
                    tt(ar[:, :, 1, :], n3(rx[:, :]), n3(t_d[:, :]), MUL).then_inc(s("rt_done"), 1)
                    dve.wait_ge(s("rt_done"), c + 1)
                    stt(rx[:, :], rx[:, :], col("r_k", c), t_e[:, :], MUL, MUL).then_inc(s("rk_done"), 1)

            def bonus(c):
                dve.wait_ge(s("bonus_mm"), c + 1)
                dve.wait_ge(*evacuated(g1(3 + 3 * c)))
                tt(ym[:, c, :], vT[:, :], bank(6), MUL).then_inc(s("bonus_done"), 1)

            def scores(c, i):
                if i == 0:
                    if c:
                        dve.wait_ge(s("y_mm"), 4 * c)
                    dve.wait_ge(s("zeroed"), 5)
                for yy in range(2 * i, 2 * i + 2) if i < 4 else ():
                    dve.wait_ge(s("score_mm"), 8 * c + yy + 1)
                    dve.copy_predicated(SC[:, yy, :], mask("score"), bank(5 + yy % 2)).then_inc(s("score_done"), 1)
                if i != 4:
                    return
                dve.wait_ge(s("L_mm"), c + 1)
                dve.wait_ge(s("x_id"), 2 * c + 2)
                dve.wait_ge(s("score_done"), 8 * c + 8)
                q4 = lambda ap: ap.rearrange("p (y q) -> p y q", q=64)
                for h2 in range(2):
                    xx = X[:, h2:8:2, :].rearrange("p y (q h) -> p y q h", h=2)[:, :, :, 0]
                    dve.copy_predicated(xx, q4(mask("lvlX0", 0, 256)), q4(bank(3 + h2, 0, 256)))
                for b in range(2):
                    lt = SC[:, 4 * b:4 * b + 4, 0:P].rearrange("p y (q h) -> p y q h", h=2)[:, :, :, 1]
                    xt = XT[:, 4 * b:4 * b + 4, :].rearrange("p y (q h) -> p y q h", h=2)[:, :, :, 1]
                    dve.copy_predicated(xt, q4(mask("lvlXT0", 0, 256)), lt).then_inc(s("x_init"), 1)

            def dx(c, lv, b):
                B = 1 << lv
                at = (6 * c + lv - 1) * 2 + b
                dve.wait_ge(s("dx_mm"), at + 1)
                if lv < LEVELS - 1:
                    dve.copy_predicated(half_of(X, b, B, 0), as2(mask(f"lvlX{lv}", 0, 256), B),
                                        as2(bank(4 + b, 0, 256), B))
                dve.copy_predicated(half_of(XT, b, B, 1), as2(mask(f"lvlXT{lv}", 0, 256), B),
                                    as2(bank(4 + b, 256, 512), B)).then_inc(s("xt_upd"), 1)

            def st(c, n):
                if n == TT - 1:
                    return
                at = 3 * c + n
                dve.wait_ge(s("dec_done"), c + 1)
                if n:
                    dve.wait_ge(s("Sp_done"), at)
                    ts(Sd[:, :], Sp[:, :], dec[:, c % 2, n:n + 1], None, MUL).then_inc(s("Sd_done"), 1)
                else:
                    if c:
                        dve.wait_ge(s("Sp_done"), at)
                    dve.memset(Sd[:, :], 0.0).then_inc(s("Sd_done"), 1)
                dve.wait_ge(s("s_mm"), at + 1)
                dve.wait_ge(s("Sd_done"), at + 1)
                if n or c:
                    dve.wait_ge(s("y_mm"), 4 * c + n)
                if n:
                    dve.wait_ge(s("y_mm"), 4 * c + n + 1)
                stt(Sp[:, :], bank(2, 256, 320), dec[:, c % 2, n:n + 1], Sd[:, :], MUL, ADD).then_inc(s("Sp_done"), 1)

            def post(c, i):
                if i == 0:
                    dve.wait_ge(s("ymean_mm"), c + 1)
                    stt(y[:, :], bank(7), -1.0 / 64, y[:, :], MUL, ADD).then_inc(s("yc_done"), 1)
                if i == 2:
                    dve.wait_ge(s("ysd_done"), c + 1)
                    dve.reciprocal(ysq[:, :], ysq[:, :]).then_inc(s("yrs_done"), 1)
                    dve.wait_ge(s("yrs_done"), c + 1)
                    tt(y[:, :], y[:, :], ysq[:, :], MUL).then_inc(s("yn_done"), 1)
                if i == 3:
                    dve.wait_ge(s("yg_done"), c + 1)
                    dve.wait_ge(s("bonus_done"), c + 1)
                    tt(y[:, :], y[:, :], ym[:, c, :], ADD).then_inc(s("yb_done"), 1)
                    dve.wait_ge(s("yb_done"), c + 1)
                    dve.wait_ge(s("gate_mm"), c + 1)
                    tt(ym[:, c, :], y[:, :], bank(7), MUL).then_inc(s("ym_done"), 1)

            def taps(c, a, b):
                for j in range(a, b):
                    if j == 0:
                        dve.wait_ge(*evacuated(g1(15 + 2 * c)))
                        ts(cv[:, c, :], zpad[:, 0:SEQ], col("conv_w", TAPS * c), col("conv_b", c), MUL, ADD)\
                            .then_inc(s("tap_done"), 1)
                    else:
                        dve.wait_ge(s("tap_done"), TAPS * c + j)
                        stt(cv[:, c, :], zpad[:, j:j + SEQ], col("conv_w", TAPS * c + j), cv[:, c, :], MUL, ADD)\
                            .then_inc(s("tap_done"), 1)

            def conv_ln(i):
                if i == 1:
                    dve.wait_ge(s("cmean_mm"), 1)
                    for c in range(CT):
                        stt(cv[:, c, :], bank(4), -1.0 / 512, cv[:, c, :], MUL, ADD).then_inc(s("cc_done"), 1)
                if i == 3:
                    dve.wait_ge(s("csd_done"), 1)
                    dve.reciprocal(t_c[:, :], t_c[:, :]).then_inc(s("crs_done"), 1)
                if i == 4:
                    dve.wait_ge(s("crs_done"), 1)
                    for c in range(CT):
                        tt(cv[:, c, :], cv[:, c, :], t_c[:, :], MUL).then_inc(s("cn_done"), 1)

            def m(i):
                k = M_TILES[i]
                dve.wait_ge(s("m_hi_done"), KD + i + 1)
                src = ym[:, k, :] if k < CT else cv[:, k - CT, :]
                tt(h_lo[:, k, :], src, F(h_hi[:, k, :]), SUB).then_inc(s("m_lo_done"), 1)

            steps = {"evac_v": evac, "decay_v": decay, "ks_v": ks, "dyn": dyn, "bonus": bonus, "scores": scores,
                     "dx": dx, "st": st, "post_v": post, "taps": taps, "conv_ln": conv_ln, "m": m}
            for name, *a in ORDER1:
                if name in steps:
                    steps[name](*a)
            residual(N_OUT1, 3)
            norm(3)
            mlp(1)
            norm(4)


def _both(w, a, b):
    t = np.stack([w[:, a], w[:, b]])
    return t.reshape(2, KD, P, P).transpose(2, 0, 1, 3).reshape(P, 2048)


def _tok(w, c0):
    return w[:, c0:c0 + 256].reshape(KD, P, 256).transpose(1, 0, 2).reshape(P, 2048)


def _down(w, half, d):
    r = HALF_K * P
    return w[half * r:(half + 1) * r, d * P:d * P + P].reshape(HALF_K, P, P).transpose(1, 0, 2).reshape(P, 2048)


def _weights(i):
    R = lambda c: list(range(c, c + P))
    e, o = i["even_w_in"][0], i["odd_w_in"][0]
    out = []
    alr = list(range(1536, 1552)) * 8
    out.append(_both(e, alr, alr))
    out += [_tok(e, 512), _tok(e, 768), _both(e, R(256), R(384)), _both(e, R(0), R(128))]
    out += [_tok(e, 2064), _tok(e, 2320), _tok(e, 1552), _tok(e, 1808), _tok(e, 1024), _tok(e, 1280)]

    def rest(w_out, up, down):
        r = [_both(w_out, R(256 * n), R(256 * n + 128)) for n in range(4)]
        for half in range(2):
            r += [_both(up, R(2048 * half + 256 * n), R(2048 * half + 256 * n + 128)) for n in range(8)]
            r += [_down(down, half, d) for d in range(KD)]
        return r
    out += rest(i["even_w_out"][0], i["w_up"][0], i["w_down"][0])
    xw, xg = list(range(1536, 1600)), list(range(1600, 1696))
    tiles = {0: xw + xw, 1: xg + xg[:32]}
    for c in range(CT):
        tiles[2 + 3 * c] = R(512 + P * c)
        tiles[3 + 3 * c] = R(1024 + P * c)
        tiles[4 + 3 * c] = R(P * c)
        tiles[14 + 2 * c] = R(1696 + 512 + P * c)
        tiles[15 + 2 * c] = R(1696 + P * c)
    out += [_both(o, tiles[ROWS[2 * n]], tiles[ROWS[2 * n + 1]]) for n in range(11)]
    out += rest(i["odd_w_out"][0], i["w_up"][1], i["w_down"][1])
    return np.ascontiguousarray(np.stack(out))


def _cols(i):
    c = np.zeros((P, NCOL), np.float32)

    def put(name, v):
        at, n = COLS[name]
        c[:, at:at + n] = v
    v = lambda a: a.reshape(-1, P).T
    mu = i["rwkv_mu"][0]
    put("norm_mix0", v(i["norm_mix"][0])), put("norm_mix1", v(i["norm_mix"][1]))
    put("norm_ffn0", v(i["norm_ffn"][0])), put("norm_ffn1", v(i["norm_ffn"][1]))
    put("norm_final", v(i["norm_final"]))
    put("b_alpha", v(i["gla_b_alpha"][0])), put("gla_norm", v(i["gla_norm"][0]))
    put("sgu_b", i["sgu_b"][0].T)
    low0, low1 = mu[1536:1600], mu[1600:1696]
    put("mu_low", np.stack([np.concatenate([low0, low0]), np.concatenate([low1, low1[:32]])]).T)
    put("mu_r", v(mu[0:512])), put("mu_k", v(mu[512:1024])), put("mu_v", v(mu[1024:1536]))
    put("w0", v(i["rwkv_w0"][0])), put("a0", v(i["rwkv_a0"][0]))
    put("k_k", v(i["rwkv_k_k"][0])), put("k_a", v(i["rwkv_k_a"][0])), put("r_k", v(i["rwkv_r_k"][0].reshape(-1)))
    put("gn_g", v(i["rwkv_gn_g"][0])), put("gn_b", v(i["rwkv_gn_b"][0]))
    put("conv_b", v(i["conv_b"][0])), put("ln_g", v(i["conv_ln_g"][0])), put("ln_b", v(i["conv_ln_b"][0]))
    put("conv_w", i["conv_w"][0].reshape(TAPS, CT, P).transpose(2, 1, 0).reshape(P, CT * TAPS))
    return c


def _masks():
    p, t = np.arange(P)[:, None], np.arange(P)[None, :]
    m = np.zeros((P, NSRC), np.float32)

    def put(name, v):
        at, n = MSRC[name]
        m[:, at:at + n] = v
    put("gla", (p // 64 == t // 64) & (p <= t))
    put("score", np.concatenate([p < t, p <= t], 1))
    put("reset64", t % GLA_CHUNK != 0)
    put("reset128", t % P != 0)
    for lv in range(LEVELS):
        B = 1 << lv
        pair = (np.arange(64) // B)[None, :]
        put(f"lvlX{lv}", (p // (2 * B) == pair) & (p % (2 * B) >= B))
        put(f"lvlXT{lv}", (p // (2 * B) == pair) & (p % (2 * B) < B))
    return m


def kernel(**inputs):
    import concourse.bacc as bacc
    from concourse.bass_utils import run_bass_kernel_spmd as run

    i = {k: np.asarray(v) for k, v in inputs.items()}
    xT = np.ascontiguousarray(i["x"][0].T.reshape(KD, P, SEQ).transpose(1, 0, 2))
    p, t = np.arange(P)[:, None], np.arange(P)[None, :]
    mats = np.stack([p == t, p == p + 0 * t, p // 64 == t // 64], 1).astype(np.float32)
    sgu_ln = np.ascontiguousarray(np.broadcast_to(np.stack([i["sgu_ln_g"][0], i["sgu_ln_b"][0]]), (P, 2, 512)))
    sgu_w = np.ascontiguousarray(i["sgu_w"][0].transpose(2, 0, 1))
    low_w = np.zeros((P, 2, 512), np.float32)
    low_w[0:32, 0], low_w[32:64, 0], low_w[0:96, 1] = i["rwkv_w2"][0], i["rwkv_a2"][0], i["rwkv_g2"][0]
    arrays = {"xT": xT, "weights": _weights(i), "cols": _cols(i), "mats": mats, "masks": _masks(), "sgu_ln": sgu_ln,
              "sgu_w": sgu_w, "alpha_w": np.ascontiguousarray(i["gla_w_alpha2"][0]), "low_w": low_w}
    nc = bacc.Bacc("TRN2", target_bir_lowering=False, num_devices=1)
    args = [nc.dram_tensor("in_" + k, a.shape, mybir.dt.from_np(a.dtype), kind="ExternalInput").ap()
            for k, a in arrays.items()]
    args.append(nc.dram_tensor("outT", (P, KD, SEQ), mybir.dt.float32, kind="ExternalOutput").ap())
    build(nc, *args)
    r = run(nc, [{"in_" + k: a for k, a in arrays.items()}], core_ids=[0])
    return np.ascontiguousarray(r.results[0]["outT"].transpose(1, 0, 2).reshape(D, SEQ).T).reshape(1, SEQ, D)
```
